# Optimizing a Trainium2 kernel written in Bass

```python
import math
import jax, jax.numpy as jnp
from jax import lax
import numpy as np

D_MODEL = 1024
BATCH = 1
SEQ = 256
DEPTH = 1

HEAD_DIM = 64
N_DIFF_HEADS = D_MODEL // HEAD_DIM // 2
DIFF_QK_DIM = HEAD_DIM // 2
N_DIL_HEADS = D_MODEL // HEAD_DIM // 2
N_HEADS_TOTAL = N_DIFF_HEADS + N_DIL_HEADS
MIX_WIDTH = N_HEADS_TOTAL * HEAD_DIM
DIL_PATTERNS = ((128, 1), (512, 4), (2048, 16))
Q_BLOCK = 128
N_EXPERTS = 32
TOP_K = 4
D_FF = D_MODEL
SWIGLU_LIMIT = 7.0
SWIGLU_ALPHA = 1.702
MOE_BLOCK = 256
NORM_EPS = 1e-5

DIFF_Q_COLS = N_DIFF_HEADS * 2 * DIFF_QK_DIM
DIFF_K_COLS = N_DIFF_HEADS * 2 * DIFF_QK_DIM
DIFF_V_COLS = N_DIFF_HEADS * HEAD_DIM
DIL_Q_COLS = N_DIL_HEADS * HEAD_DIM
DIL_K_COLS = N_DIL_HEADS * HEAD_DIM
DIL_V_COLS = N_DIL_HEADS * HEAD_DIM
IN_COLS = DIFF_Q_COLS + DIFF_K_COLS + DIFF_V_COLS + DIL_Q_COLS + DIL_K_COLS + DIL_V_COLS

kernel_name = "hybrid_diffattn_dilated_moe_block"

def rms_norm(x, w):
    xf = x.astype(jnp.float32)
    y = xf * lax.rsqrt(jnp.mean(xf * xf, axis=-1, keepdims=True) + NORM_EPS)
    return (y * w.astype(jnp.float32)).astype(x.dtype)

def alibi_slopes(n):
    return jnp.exp2(-8.0 * jnp.arange(1, n + 1, dtype=jnp.float32) / n)

def diff_attention(q, k, v, slopes, lam):
    S = q.shape[1]
    scale = DIFF_QK_DIM ** -0.5
    outs = []
    for i in range(S // Q_BLOCK):
        q0 = i * Q_BLOCK
        kend = q0 + Q_BLOCK
        qb, kb, vb = q[:, q0:kend], k[:, :kend], v[:, :kend]
        s = jnp.einsum('bqhmd,bkhmd->bhmqk', qb, kb,
                       preferred_element_type=jnp.float32) * scale
        dist = (q0 + jnp.arange(Q_BLOCK))[:, None] - jnp.arange(kend)[None, :]
        s = s - slopes[None, :, None, None, None] * dist.astype(jnp.float32)
        s = jnp.where(dist >= 0, s, -jnp.inf)
        p = jax.nn.softmax(s, axis=-1)
        pd = p[:, :, 0] - lam * p[:, :, 1]
        outs.append(jnp.einsum('bhqk,bkhd->bqhd', pd.astype(v.dtype), vb))
    return jnp.concatenate(outs, axis=1)

def dilated_pattern(q, k, v, slopes, window, dilation):
    B, S, H, Dh = q.shape
    L = S // dilation
    W = window // dilation
    nb = -(-L // W)
    Lp = nb * W
    N = B * dilation

    def to_sub(t):
        t = t.reshape(B, L, dilation, H, Dh).transpose(0, 2, 1, 3, 4).reshape(N, L, H, Dh)
        return jnp.pad(t, ((0, 0), (0, Lp - L), (0, 0), (0, 0)))

    qs, ks, vs = to_sub(q), to_sub(k), to_sub(v)
    qb = qs.reshape(N, nb, W, H, Dh)

    def kv_blocks(t):
        prev = jnp.pad(t, ((0, 0), (W, 0), (0, 0), (0, 0)))[:, :Lp].reshape(N, nb, W, H, Dh)
        cur = t.reshape(N, nb, W, H, Dh)
        return jnp.concatenate([prev, cur], axis=2)

    kb, vb = kv_blocks(ks), kv_blocks(vs)
    s = jnp.einsum('nbqhd,nbkhd->nbhqk', qb, kb,
                   preferred_element_type=jnp.float32) * (Dh ** -0.5)
    dist = jnp.arange(W)[:, None] - jnp.arange(2 * W)[None, :] + W
    kpos = (jnp.arange(nb) * W - W)[:, None] + jnp.arange(2 * W)[None, :]
    valid = ((dist >= 0) & (dist <= W))[None, :, :] & (kpos >= 0)[:, None, :]
    s = s - slopes[None, None, :, None, None] * (dist * dilation).astype(jnp.float32)
    s = jnp.where(valid[None, :, None, :, :], s, -jnp.inf)
    lse = jax.nn.logsumexp(s, axis=-1)
    p = jnp.exp(s - lse[..., None])
    o = jnp.einsum('nbhqk,nbkhd->nbqhd', p.astype(v.dtype), vb)
    o = o.reshape(N, Lp, H, Dh)[:, :L]
    o = o.reshape(B, dilation, L, H, Dh).transpose(0, 2, 1, 3, 4).reshape(B, S, H, Dh)
    lse = lse.transpose(0, 1, 3, 2).reshape(N, Lp, H)[:, :L]
    lse = lse.reshape(B, dilation, L, H).transpose(0, 2, 1, 3).reshape(B, S, H)
    return o, lse

def dilated_attention(q, k, v, slopes):
    outs, lses = [], []
    for window, dilation in DIL_PATTERNS:
        o, l = dilated_pattern(q, k, v, slopes, window, dilation)
        outs.append(o)
        lses.append(l)
    wts = jax.nn.softmax(jnp.stack(lses, axis=0), axis=0)
    o = jnp.sum(wts[..., None] * jnp.stack(outs, axis=0).astype(jnp.float32), axis=0)
    return o.astype(q.dtype)

def moe_ffn(h, router_w, router_b, w_gate_up, b_gate_up, w_down, b_down):
    Bb, S, D = h.shape
    T = Bb * S
    xf = h.reshape(T, D)
    logits = (xf @ router_w + router_b).astype(jnp.float32)
    top_v, top_i = lax.top_k(logits, TOP_K)
    gates = jax.nn.softmax(top_v, axis=-1)
    flat_e = top_i.reshape(-1)
    flat_t = jnp.arange(T * TOP_K, dtype=jnp.int32) // TOP_K
    flat_g = gates.reshape(-1)
    order = jnp.argsort(flat_e)
    se = flat_e[order]
    counts = jnp.bincount(flat_e, length=N_EXPERTS)
    starts = jnp.cumsum(counts) - counts
    pcounts = (counts + MOE_BLOCK - 1) // MOE_BLOCK * MOE_BLOCK
    pends = jnp.cumsum(pcounts)
    pstarts = pends - pcounts
    dest = pstarts[se] + jnp.arange(T * TOP_K) - starts[se]
    n_blocks = -(-(T * TOP_K + N_EXPERTS * (MOE_BLOCK - 1)) // MOE_BLOCK)
    R = n_blocks * MOE_BLOCK
    row_tok = jnp.full((R,), T, dtype=jnp.int32).at[dest].set(flat_t[order])
    row_gate = jnp.zeros((R,), dtype=h.dtype).at[dest].set(flat_g[order].astype(h.dtype))
    block_e = jnp.minimum(jnp.searchsorted(pends, jnp.arange(n_blocks) * MOE_BLOCK, side='right'),
                          N_EXPERTS - 1)
    x_pad = jnp.concatenate([xf, jnp.zeros((1, D), xf.dtype)], axis=0)

    def expert_block(args):
        tok, g, e = args
        xb = x_pad[tok]
        gu = xb @ w_gate_up[e] + b_gate_up[e]
        gate, up = gu[:, :D_FF], gu[:, D_FF:]
        gate = jnp.minimum(gate, SWIGLU_LIMIT)
        up = jnp.clip(up, -SWIGLU_LIMIT, SWIGLU_LIMIT)
        act = (up + 1.0) * (gate * jax.nn.sigmoid(SWIGLU_ALPHA * gate))
        return (act @ w_down[e] + b_down[e]) * g[:, None]

    out_rows = lax.map(expert_block, (row_tok.reshape(n_blocks, MOE_BLOCK),
                                      row_gate.reshape(n_blocks, MOE_BLOCK), block_e))
    y = jax.ops.segment_sum(out_rows.reshape(R, D), row_tok, num_segments=T + 1)[:T]
    return y.reshape(Bb, S, D)

def setup_inputs(seed: int = 0) -> dict:
    key = jax.random.key(seed)
    ks = jax.random.split(key, 18)
    f32 = jnp.float32
    nrm = lambda k, shape, scale: jax.random.normal(k, shape, f32) * scale
    return {
        "x": nrm(ks[0], (BATCH, SEQ, D_MODEL), 1.0),
        "attn_norm_w": 1.0 + nrm(ks[1], (DEPTH, D_MODEL), 0.02),
        "w_in": nrm(ks[2], (DEPTH, D_MODEL, IN_COLS), D_MODEL ** -0.5),
        "diff_lambda_q1": nrm(ks[3], (DEPTH, DIFF_QK_DIM), 0.1),
        "diff_lambda_k1": nrm(ks[4], (DEPTH, DIFF_QK_DIM), 0.1),
        "diff_lambda_q2": nrm(ks[5], (DEPTH, DIFF_QK_DIM), 0.1),
        "diff_lambda_k2": nrm(ks[6], (DEPTH, DIFF_QK_DIM), 0.1),
        "diff_subln_w": 1.0 + nrm(ks[7], (DEPTH, HEAD_DIM), 0.02),
        "w_out": nrm(ks[8], (DEPTH, MIX_WIDTH, D_MODEL), MIX_WIDTH ** -0.5),
        "ffn_norm_w": 1.0 + nrm(ks[9], (DEPTH, D_MODEL), 0.02),
        "router_w": nrm(ks[10], (DEPTH, D_MODEL, N_EXPERTS), D_MODEL ** -0.5),
        "router_b": nrm(ks[11], (DEPTH, N_EXPERTS), 0.01),
        "w_gate_up": nrm(ks[12], (DEPTH, N_EXPERTS, D_MODEL, 2 * D_FF), D_MODEL ** -0.5),
        "b_gate_up": nrm(ks[13], (DEPTH, N_EXPERTS, 2 * D_FF), 0.01),
        "w_down": nrm(ks[14], (DEPTH, N_EXPERTS, D_FF, D_MODEL), D_FF ** -0.5),
        "b_down": nrm(ks[15], (DEPTH, N_EXPERTS, D_MODEL), 0.01),
        "final_norm_w": 1.0 + nrm(ks[16], (D_MODEL,), 0.02),
    }

def reference(x, attn_norm_w, w_in, diff_lambda_q1, diff_lambda_k1, diff_lambda_q2,
              diff_lambda_k2, diff_subln_w, w_out, ffn_norm_w, router_w, router_b,
              w_gate_up, b_gate_up, w_down, b_down, final_norm_w):
    B, S, _ = x.shape
    slopes = alibi_slopes(N_HEADS_TOTAL)
    diff_slopes = slopes[0::2]
    dil_slopes = slopes[1::2]
    split_at = list(np.cumsum([DIFF_Q_COLS, DIFF_K_COLS, DIFF_V_COLS,
                               DIL_Q_COLS, DIL_K_COLS])[:])
    for l in range(DEPTH):
        h = rms_norm(x, attn_norm_w[l])
        proj = h @ w_in[l]
        dq, dk, dv, lq, lk, lv = jnp.split(proj, split_at, axis=-1)
        dq = dq.reshape(B, S, N_DIFF_HEADS, 2, DIFF_QK_DIM)
        dk = dk.reshape(B, S, N_DIFF_HEADS, 2, DIFF_QK_DIM)
        dv = dv.reshape(B, S, N_DIFF_HEADS, HEAD_DIM)
        lam_init = 0.8 - 0.6 * math.exp(-0.3 * l)
        lam = (jnp.exp(jnp.sum(diff_lambda_q1[l] * diff_lambda_k1[l]).astype(jnp.float32))
               - jnp.exp(jnp.sum(diff_lambda_q2[l] * diff_lambda_k2[l]).astype(jnp.float32))
               + lam_init)
        o_diff = diff_attention(dq, dk, dv, diff_slopes, lam)
        o_diff = rms_norm(o_diff, diff_subln_w[l]) * (1.0 - lam_init)
        lq = lq.reshape(B, S, N_DIL_HEADS, HEAD_DIM)
        lk = lk.reshape(B, S, N_DIL_HEADS, HEAD_DIM)
        lv = lv.reshape(B, S, N_DIL_HEADS, HEAD_DIM)
        o_dil = dilated_attention(lq, lk, lv, dil_slopes)
        mix = jnp.concatenate([o_diff.reshape(B, S, DIFF_V_COLS),
                               o_dil.reshape(B, S, DIL_V_COLS)], axis=-1)
        x = x + mix @ w_out[l]
        x = x + moe_ffn(rms_norm(x, ffn_norm_w[l]), router_w[l], router_b[l],
                        w_gate_up[l], b_gate_up[l], w_down[l], b_down[l])
    return rms_norm(x, final_norm_w)


_drawn_inputs = setup_inputs


def setup_inputs(seed=0):
    import zlib

    import numpy as np

    out = dict(_drawn_inputs(seed))
    spreads = {}
    factors = {'b_gate_up': 8.0, 'b_down': 8.0, 'final_norm_w': 2.858}
    for name, (base, spread) in spreads.items():
        noise = np.random.default_rng([zlib.crc32(name.encode()), seed]).standard_normal(out[name].shape)
        drawn = base * np.exp(spread * noise) if base else spread * noise
        out[name] = __import__('jax').numpy.asarray(drawn.astype(out[name].dtype))
    for name, factor in factors.items():
        out[name] = (out[name] * factor).astype(out[name].dtype)
    return out
```

```python
import numpy as np
import concourse.bass as bass
from concourse import mybir
from concourse.alu_op_type import AluOpType as ALU
from contextlib import ExitStack

F32 = mybir.dt.float32
I32 = mybir.dt.int32
U32 = mybir.dt.uint32
ACT = mybir.ActivationFunctionType
AX = mybir.AxisListType

P = 128
T, D = 256, 1024
TT = T // P
KT = D // P
HD = 64
NH = 8
DK = HD // 2
EPS = 1e-5
LAM_INIT = 0.8 - 0.6
NE, TOPK, FF = 32, 4, 1024
LIMIT, ALPHA = 7.0, 1.702
CAP = 64
PAIRS = NE // 2
ROUNDS = T // CAP
SLOPES = [2.0 ** (-8.0 * (i + 1) / (2 * NH)) for i in range(2 * NH)]
FAR = 1e30
WS = 2048
GUN, DNN = 16, 4


def moe_block(nc, x, attn_norm_w, w_in, lq1, lk1, lq2, lk2, subln_w, w_out, ffn_norm_w, router_w, router_b,
              w_gate_up, b_gate_up, w_down, b_down, final_norm_w, out):
    ctx = ExitStack()
    with ctx:
        def sb(name, shape, dt=F32):
            return ctx.enter_context(nc.sbuf_tensor(name, shape, dt))

        def sem(name):
            return ctx.enter_context(nc.semaphore(name))

        gu_ring = sb("gu_ring", [P, GUN, WS])
        dn_ring = sb("dn_ring", [P, DNN, WS])
        xres = sb("xres", [P, TT, D])
        hmix = sb("hmix", [P, TT, D])
        shared = sb("shared", [P, 6528])
        posm = sb("posm", [P, TT, 2 + NE * ROUNDS + 2])
        gates = sb("gates", [P, TT, 2 + NE])
        bguT = sb("bguT", [P, 2 * KT, NE])
        bdT = sb("bdT", [P, KT, NE])
        ident = sb("ident", [P, P])
        iota = sb("iota", [P, CAP])
        prm = sb("prm", [P, 17])
        rb = sb("rb", [P, NE])
        st = sb("st", [P, 64])
        rounds = sb("rounds", [P, 1], I32)

        hT = gu_ring[:, 12, :].rearrange("p (k t) -> p k t", k=KT)
        qkT = gu_ring[:, 13:15, :].rearrange("p s (m t) -> p (s m) t", t=T)
        vS = gu_ring[:, 15, :].rearrange("p (a c) -> p a c", a=TT)
        bgu_rows = dn_ring[0:NE, 0, :]
        bd_rows = dn_ring[0:NE, 1, 0:D]

        def part(a, n):
            return shared[:, a:a + n]

        mixT = part(0, 2048).rearrange("p (k t) -> p k t", k=KT)
        h2T = mixT
        scores = [part(2048 + 768 * i, 768).rearrange("p (m j) -> p m j", m=2) for i in range(2)]
        probs = [part(3584 + 384 * i, 384) for i in range(2)]
        probsT = [part(4352 + 384 * i, 384) for i in range(2)]
        dist_diff = part(5120, 384)
        dist_dil = part(5504, 384)
        mult = part(5888, 384)
        rw = part(6272, 256).rearrange("p (k e) -> p k e", k=KT)
        tri = part(5120, P)
        ones = part(5120 + P, P)
        lam_rows = part(2048, 4 * DK).rearrange("p (v d) -> p v d", v=4)
        prm_rows = part(3584, P)[0:17, :]
        dist_int = part(4352, 384).bitcast(I32)
        mod_int = part(3584 + P, 384).bitcast(I32)
        sel_k = part(2048, 256).rearrange("p (a k e) -> p a k e", a=TT, k=TOPK)
        selg_k = part(2304, 256).rearrange("p (a k e) -> p a k e", a=TT, k=TOPK)
        chosen = part(2560, TT * NE).rearrange("p (a e) -> p a e", a=TT)
        logits = part(2624, TT * NE).rearrange("p (a e) -> p a e", a=TT)
        slot0 = part(2688, TT * NE).rearrange("p (a e) -> p a e", a=TT)
        iota_e = part(2752, NE)
        top_v = part(2784, 16).rearrange("p (a k) -> p a k", a=TT)
        top_i = part(2800, 16).bitcast(U32).rearrange("p (a k) -> p a k", a=TT)
        top_f = part(2816, 16).rearrange("p (a k) -> p a k", a=TT)
        top_e = part(2832, 16).rearrange("p (a k) -> p a k", a=TT)

        xg = part(0, 1024).rearrange("p (k n) -> p k n", k=KT)
        gate_t = part(1024, 512).rearrange("p (m n) -> p m n", m=KT)
        up_t = part(1536, 512).rearrange("p (m n) -> p m n", m=KT)
        sig_t = part(2048, 512).rearrange("p (m n) -> p m n", m=KT)
        act_t = part(2560, 512).rearrange("p (m n) -> p m n", m=KT)
        yT = part(3072, 1024).rearrange("p (m n) -> p m n", m=KT)
        yrow = part(4096, 1024)
        combT = part(5120, 256)
        sel = part(5376, 256).rearrange("p (a e n) -> p a e n", a=TT, e=2)
        selg = part(5632, 256).rearrange("p (a e n) -> p a e n", a=TT, e=2)

        psum = ctx.enter_context(nc.psum_tensor("psum", [P, 8, 512], F32))
        bank = [psum[:, i, :] for i in range(8)]

        x_in = sem("x_in")
        small_in = sem("small_in")
        bias_in = sem("bias_in")
        rw_in = sem("rw_in")
        w_in_in = [sem(f"w_in_in{i}") for i in range(12)]
        w_out_in = [sem(f"w_out_in{i}") for i in range(4)]
        gu_in = [sem(f"gu_in{i}") for i in range(GUN)]
        dn_in = [sem(f"dn_in{i}") for i in range(DNN)]
        fw_in = sem("fw_in")
        out_done = sem("out_done")
        pool_step = sem("pool_step")
        tables = sem("tables")
        tri_made = sem("tri_made")
        dve_step = sem("dve_step")
        ms_ready = sem("ms_ready")
        rs_ready = sem("rs_ready")
        consts = sem("consts")
        h_ready = sem("h_ready")
        prmT_done = sem("prmT_done")
        prm_ready = sem("prm_ready")
        biasT_done = sem("biasT_done")
        biasT_read = sem("biasT_read")
        hT_done = sem("hT_done")
        hT_ready_v = sem("hT_ready_v")
        hT_ready_a = sem("hT_ready_a")
        w_in_used = sem("w_in_used")
        proj_ready_v = sem("proj_ready_v")
        proj_ready_a = sem("proj_ready_a")
        lam_sum = sem("lam_sum")
        lam_exp = sem("lam_exp")
        scores_done = sem("scores_done")
        scores_read = sem("scores_read")
        max_ready = sem("max_ready")
        exp_done = sem("exp_done")
        probs_ready = sem("probs_ready")
        probsT_done = sem("probsT_done")
        probsT_ready = sem("probsT_ready")
        pv_done = sem("pv_done")
        pv_read = sem("pv_read")
        mix_ready = sem("mix_ready")
        mixT_done = sem("mixT_done")
        mixT_ready = sem("mixT_ready")
        oproj_done = sem("oproj_done")
        h2_ready = sem("h2_ready")
        h2T_done = sem("h2T_done")
        h2T_ready = sem("h2T_ready")
        logits_done = sem("logits_done")
        top_ready = sem("top_ready")
        top_exp = sem("top_exp")
        chosen_ready = sem("chosen_ready")
        pos_done = sem("pos_done")
        rounds_ready = sem("rounds_ready")
        sel_ready = sem("sel_ready")
        selg_ready = sem("selg_ready")
        gather_done = sem("gather_done")
        xg_ready = sem("xg_ready")
        gu_used = sem("gu_used")
        dn_used = sem("dn_used")
        gate_ready = sem("gate_ready")
        sig_ready = sem("sig_ready")
        act_ready = sem("act_ready")
        yT_ready = sem("yT_ready")
        yT_turned = sem("yT_turned")
        yrow_ready = sem("yrow_ready")
        comb_done = sem("comb_done")
        comb_added = sem("comb_added")
        dve_loop = sem("dve_loop")

        tok = "b (a p) d -> p (b a) d"
        block = ctx.enter_context(nc.Block())

        @block.sync
        def _(sp):
            xv = x.rearrange(tok, p=P)
            for a in range(TT):
                sp.dma_start(xres[:, a, :], xv[:, a, :]).then_inc(x_in, 16)
            w_in_v = w_in.rearrange("o (k p) c -> p (o k) c", p=P)
            for g in range(3):
                for q in range(4):
                    s = 4 * g + q
                    sp.dma_start(gu_ring[:, s, :].rearrange("p (k c) -> p k c", k=2),
                                 w_in_v[:, 2 * q:2 * q + 2, D * g:D * (g + 1)]).then_inc(w_in_in[s], 16)
            w_out_v = w_out.rearrange("o (k p) c -> p (o k) c", p=P)
            sp.wait_ge(biasT_done, 2)
            for q in range(4):
                sp.dma_start(dn_ring[:, q, :].rearrange("p (k c) -> p k c", k=2),
                             w_out_v[:, 2 * q:2 * q + 2, :]).then_inc(w_out_in[q], 16)

            gu_v = w_gate_up[0, :, :, :].rearrange("e (k p) c -> p e k c", p=P)
            dn_v = w_down[0, :, :, :].rearrange("e (k p) c -> p e k c", p=P)

            def load_gu(e, half, k):
                s = 8 * half + k
                sp.dma_start(gu_ring[:, s, :].rearrange("p (e c) -> p e c", e=1),
                             gu_v[:, bass.ds(e, 1), k, :]).then_inc(gu_in[s], 16)

            def load_dn(e, q):
                sp.dma_start(dn_ring[:, q:q + 1, :].rearrange("p e (k c) -> p e k c", k=2),
                             dn_v[:, bass.ds(e, 1), 2 * q:2 * q + 2, :]).then_inc(dn_in[q], 16)

            for s in range(GUN):
                if s < 12:
                    sp.wait_ge(w_in_used, s + 1)
                elif s == 12:
                    sp.wait_ge(w_in_used, 12)
                elif s < 15:
                    sp.wait_ge(scores_done, 2 * NH)
                else:
                    sp.wait_ge(pv_done, 2 * NH)
                load_gu(s // 8, s // 8, s % 8)
            for q in range(DNN):
                sp.wait_ge(oproj_done, 2 * q + 2)
                load_dn(0, q)
            for q in range(DNN):
                sp.wait_ge(dn_used, q + 1)
                load_dn(1, q)
            sp.wait_ge(rounds_ready, 1)
            n = sp.value_load(rounds[0:1, 0:1], min_val=1, max_val=ROUNDS)
            with sp.Fori(1, n * PAIRS) as j:
                for half in range(2):
                    e = (j % PAIRS) * 2 + half
                    for k in range(KT):
                        sp.wait_ge(gu_used, j * GUN + (8 * half + k + 1 - GUN))
                        load_gu(e, half, k)
                    for q in range(DNN):
                        sp.wait_ge(dn_used, j * (2 * DNN) + (DNN * half + q + 1 - DNN))
                        load_dn(e, q)
            sp.wait_ge(gu_used, n * (PAIRS * GUN))
            sp.dma_start(gu_ring[:, 0, 0:D], final_norm_w.rearrange("(a d) -> a d", a=1).broadcast_to([P, D]))\
                .then_inc(fw_in, 16)
            out_v = out.rearrange(tok, p=P)
            for a in range(TT):
                sp.wait_ge(h_ready, TT + a + 1)
                sp.dma_start(out_v[:, a, :], hmix[:, a, :]).then_inc(out_done, 16)
            sp.wait_ge(out_done, 16 * TT)

        @block.gpsimd
        def _(pool):
            count = [0]

            def link(ins):
                count[0] += 1
                ins.then_inc(pool_step, 1)
                pool.wait_ge(pool_step, count[0])

            def eye(m):
                link(nc.gpsimd.memset(m, 0.0))
                return nc.gpsimd.affine_select(out=m, in_=m, compare_op=ALU.not_equal, fill=1.0, base=0,
                                               pattern=[[-1, P]], channel_multiplier=1)

            eye(ident[:, :]).then_inc(tables, 1)
            for dst in (dist_diff, dist_int):
                nc.gpsimd.iota(dst[:, T:T + P], pattern=[[-1, P]], base=0, channel_multiplier=1,
                               allow_small_or_imprecise_dtypes=True).then_inc(tables, 1)
                nc.gpsimd.iota(dst[:, 0:T], pattern=[[-1, T]], base=P, channel_multiplier=1,
                               allow_small_or_imprecise_dtypes=True).then_inc(tables, 1)
            nc.gpsimd.iota(iota[:, :], pattern=[[1, CAP]], base=0, channel_multiplier=0,
                           allow_small_or_imprecise_dtypes=True).then_inc(tables, 1)

            def rsqrt(n, src, dst):
                pool.wait_ge(ms_ready, n)
                nc.gpsimd.tensor_tensor(dst, src, st[:, 62:63].broadcast_to(list(dst.shape)), ALU.pow)\
                    .then_inc(rs_ready, 1)

            pool.wait_ge(consts, 1)
            rsqrt(1, st[:, 0:2], st[:, 2:4])
            for i in range(NH // 2):
                rsqrt(2 + i, st[:, 16:20], st[:, 20:24])
            pool.wait_ge(probs_ready, 2 * NH)
            link(nc.gpsimd.memset(ones, 1.0))
            nc.gpsimd.affine_select(out=tri, in_=ones, compare_op=ALU.is_gt, fill=0.0, base=0,
                                    pattern=[[1, P]], channel_multiplier=-1).then_inc(tri_made, 1)
            rsqrt(2 + NH // 2, st[:, 0:2], st[:, 2:4])
            rsqrt(3 + NH // 2, st[:, 0:2], st[:, 2:4])

        @block.scalar
        def _(act):
            act.dma_start(prm_rows[0:8, :], attn_norm_w.rearrange("o (k p) -> (o k) p", p=P)).then_inc(small_in, 16)
            act.dma_start(prm_rows[8:16, :], ffn_norm_w.rearrange("o (k p) -> (o k) p", p=P)).then_inc(small_in, 16)
            for i in range(2):
                act.dma_start(prm_rows[16:17, HD * i:HD * (i + 1)], subln_w).then_inc(small_in, 16)
            act.dma_start(bgu_rows, b_gate_up[0, :, :]).then_inc(bias_in, 16)
            act.dma_start(bd_rows, b_down[0, :, :]).then_inc(bias_in, 16)
            for i, v in enumerate((lq1, lk1, lq2, lk2)):
                act.dma_start(lam_rows[:, i, :], v.broadcast_to([P, DK])).then_inc(small_in, 16)
            act.dma_start(rb[:, :], router_b.broadcast_to([P, NE])).then_inc(small_in, 16)
            act.dma_start(rw, router_w.rearrange("o (k p) e -> p (o k) e", p=P)).then_inc(rw_in, 16)

            act.wait_ge(lam_sum, 1)
            nc.scalar.activation(st[:, 6:8], st[:, 4:6], ACT.Exp).then_inc(lam_exp, 1)
            act.wait_ge(prm_ready, 1)
            act.wait_ge(hT_done, 2 * KT)
            for k in (2, 3, 6, 7):
                last = nc.scalar.activation(hT[:, k, :], bank[4 + k // 2][:, T * (k % 2):T * (k % 2 + 1)], ACT.Copy,
                                            scale=prm[:, k:k + 1])
            last.then_inc(hT_ready_a, 1)
            act.wait_ge(w_in_used, 4)
            for b in range(2):
                last = nc.scalar.activation(qkT[:, 2 * b:2 * b + 2, :].rearrange("p m t -> p (m t)"), bank[b][:, :],
                                            ACT.Copy, scale=DK ** -0.5)
            last.then_inc(proj_ready_a, 1)
            act.wait_ge(w_in_used, 8)
            for b in range(2):
                last = nc.scalar.activation(qkT[:, 8 + 2 * b:10 + 2 * b, :].rearrange("p m t -> p (m t)"),
                                            bank[6 + b][:, :], ACT.Copy, scale=HD ** -0.5)
            last.then_inc(proj_ready_a, 1)

            def exps(g):
                act.wait_ge(max_ready, g + 1)
                s = scores[g % 2]
                lo, z = 24 + 4 * (g % 2), 32 + 4 * (g % 2)
                maps = 2 if g < NH else 1
                for c, w, i in ((0, T, 2), (T, P, 0)):
                    for m in range(maps):
                        acc = {"accum_out": st[:, z + i + m:z + i + m + 1]} if g < NH else {}
                        last = nc.scalar.activation(s[:, m, c:c + w], s[:, m, c:c + w], ACT.Exp,
                                                    bias=st[:, lo + i + m:lo + i + m + 1], scale=-1.0, **acc)
                last.then_inc(exp_done, 1)

            def turn_probs(g):
                act.wait_ge(probsT_done, g + 1)
                if g >= 2:
                    act.wait_ge(pv_done, g - 1)
                nc.scalar.activation(probsT[g % 2], bank[6][:, 0:384], ACT.Copy).then_inc(probsT_ready, 1)

            def keep_pv(g):
                act.wait_ge(pv_done, g + 1)
                if g < NH:
                    nc.scalar.activation(hmix[:, :, HD * g:HD * (g + 1)],
                                         bank[7][:, 0:P].rearrange("p (a d) -> p a d", a=TT), ACT.Copy)\
                        .then_inc(pv_read, 1)
                else:
                    for a in range(TT):
                        last = nc.scalar.activation(hmix[:, a, HD * g:HD * (g + 1)], bank[7][:, HD * a:HD * (a + 1)],
                                                    ACT.Copy, scale=st[:, 40 + 2 * (g % 2) + a:41 + 2 * (g % 2) + a])
                    last.then_inc(pv_read, 1)

            def keep_mixT(kt):
                act.wait_ge(mixT_done, kt + 1)
                scale = prm[:, 16:17] if kt < NH // 2 else 1.0
                nc.scalar.activation(mixT[:, kt, :], bank[7][:, P:P + T], ACT.Copy, scale=scale)\
                    .then_inc(mixT_ready, 1)

            for g in range(2 * NH + 1):
                if g < 2 * NH and g != NH:
                    exps(g)
                if g >= 1:
                    turn_probs(g - 1)
                if g >= 4 and g % 2 == 0:
                    keep_mixT((g - 4) // 2)
                if g >= 1:
                    keep_pv(g - 1)
                if g == NH:
                    act.wait_ge(w_in_used, 12)
                    for a in range(TT):
                        last = nc.scalar.activation(vS[:, a, 512:D], bank[2 + a][:, :], ACT.Copy)
                    last.then_inc(proj_ready_a, 1)
                    exps(g)
            keep_mixT(NH - 1)

            act.wait_ge(top_ready, 1)
            for a in range(TT):
                last = nc.scalar.activation(top_e[:, a, 0:TOPK], top_v[:, a, 0:TOPK], ACT.Exp, bias=st[:, 46 + a:47 + a],
                                            accum_out=st[:, 48 + a:49 + a])
            last.then_inc(top_exp, 1)

            act.wait_ge(rounds_ready, 1)
            n = act.value_load(rounds[0:1, 0:1], min_val=1, max_val=ROUNDS)

            def sigmoid(v):
                act.wait_ge(gate_ready, v)
                nc.scalar.activation(sig_t, gate_t, ACT.Sigmoid, scale=ALPHA).then_inc(sig_ready, 1)

            def turn_y(v):
                act.wait_ge(yT_turned, v)
                nc.scalar.activation(combT, bank[7][:, 0:T], ACT.Copy)
                nc.scalar.activation(yrow.rearrange("p (b c) -> p b c", b=2), psum[:, 5:7, :], ACT.Copy)\
                    .then_inc(yrow_ready, 1)

            with act.Fori(0, n) as r:
                with act.Fori(0, PAIRS) as i:
                    j = r * PAIRS + i
                    sigmoid(j * 2 + 1)
                    turn_y(j + 1)
                    sigmoid(j * 2 + 2)
            turn_y(n * PAIRS + 1)

        @block.tensor
        def _(pe):
            mm = nc.tensor.matmul

            def turn(dst, src, rows=P):
                return nc.tensor.transpose(dst, src, ident[0:rows, 0:rows])

            pe.wait_ge(tables, 1)
            pe.wait_ge(small_in, 16 * 9)
            turn(bank[0][:, 0:17], prm_rows, 17).then_inc(prmT_done, 1)
            pe.wait_ge(bias_in, 32)
            for m in range(2 * KT):
                last = turn(bank[1][:, NE * m:NE * (m + 1)], bgu_rows[:, P * m:P * (m + 1)], NE)
            last.then_inc(biasT_done, 1)
            for m in range(KT):
                last = turn(bank[2][:, NE * m:NE * (m + 1)], bd_rows[:, P * m:P * (m + 1)], NE)
            last.then_inc(biasT_done, 1)
            for a in range(TT):
                pe.wait_ge(h_ready, a + 1)
                for k in range(KT):
                    c = T * (k % 2) + P * a
                    turn(bank[4 + k // 2][:, c:c + P], hmix[:, a, P * k:P * (k + 1)]).then_inc(hT_done, 1)

            def project(g, k):
                s = 4 * g + k // 2
                if k % 2 == 0:
                    pe.wait_ge(w_in_in[s], 16)
                base = D * (k % 2)
                b0 = 4 if g == 1 else 0
                last = None
                for m in range(8):
                    is_v = (g == 1 and m < 4) or (g == 2 and m >= 4)
                    if is_v:
                        continue
                    b, c = b0 + m // 2, T * (m % 2)
                    last = mm(bank[b][:, c:c + T], gu_ring[:, s, base + P * m:base + P * (m + 1)], hT[:, k, :],
                              start=(k == 0 and m % 2 == 0), stop=(k == KT - 1), skip_group_check=True)
                if g:
                    v0 = 0 if g == 1 else 512
                    for a in range(TT):
                        b = b0 + (0 if g == 1 else 2) + a
                        last = mm(bank[b][:, :], hT[:, k, P * a:P * (a + 1)],
                                  gu_ring[:, s, base + v0:base + v0 + 512], start=(k == 0), stop=(k == KT - 1))
                if k % 2:
                    last.then_inc(w_in_used, 1)

            pe.wait_ge(hT_ready_a, 1)
            pe.wait_ge(hT_ready_v, 1)
            pe.wait_ge(prm_ready, 1)
            pe.wait_ge(biasT_read, 1)
            for k in range(KT):
                project(0, k)
            for k in range(KT):
                project(1, k)

            def score(g):
                if g == 0:
                    pe.wait_ge(proj_ready_v, 2)
                    pe.wait_ge(proj_ready_a, 2)
                elif g == NH:
                    pe.wait_ge(proj_ready_v, 3)
                    pe.wait_ge(proj_ready_a, 3)
                if g >= 1:
                    pe.wait_ge(scores_read, g)
                h = g % NH
                maps = 2 if g < NH else 1
                rows = HD // maps
                for m in range(maps):
                    r0 = HD * (h % 2) + rows * m
                    tq, tk = (h // 2, 4 + h // 2) if g < NH else (8 + h // 2, 12 + h // 2)
                    q, k = qkT[r0:r0 + rows, tq, :], qkT[r0:r0 + rows, tk, :]
                    mm(bank[4 + m][:, 0:T], q[:, P:T], k, start=True, stop=True)
                    last = mm(bank[4 + m][:, T:T + P], q[:, 0:P], k[:, 0:P], start=True, stop=True)
                last.then_inc(scores_done, 1)

            def turn_probs(g):
                pe.wait_ge(probs_ready, g + 1)
                if g >= 1:
                    pe.wait_ge(probsT_ready, g)
                for b in range(3):
                    last = turn(bank[6][:, P * b:P * (b + 1)], probs[g % 2][:, P * b:P * (b + 1)])
                last.then_inc(probsT_done, 1)

            def pv(g):
                pe.wait_ge(probsT_ready, g + 1)
                if g >= 1:
                    pe.wait_ge(pv_read, g)
                if g >= 3:
                    pe.wait_ge(mixT_ready, (g - 1) // 2)
                pt = probsT[g % 2]
                v = vS[:, :, HD * g:HD * (g + 1)]
                mm(bank[7][:, 0:HD], pt[:, T:T + P], v[:, 0, :], start=True, stop=True)
                mm(bank[7][:, HD:P], pt[:, 0:P], v[:, 0, :], start=True, stop=False)
                mm(bank[7][:, HD:P], pt[:, P:T], v[:, 1, :], start=False, stop=True).then_inc(pv_done, 1)

            def turn_mix(kt):
                if kt < NH // 2:
                    pe.wait_ge(mix_ready, kt + 1)
                pe.wait_ge(pv_read, min(2 * kt + 3, 2 * NH))
                if kt >= 1:
                    pe.wait_ge(mixT_ready, kt)
                for a in range(TT):
                    last = turn(bank[7][:, P + P * a:2 * P + P * a], hmix[:, a, P * kt:P * (kt + 1)])
                last.then_inc(mixT_done, 1)

            def out_project(kt):
                pe.wait_ge(mixT_ready, kt + 1)
                if kt % 2 == 0:
                    pe.wait_ge(w_out_in[kt // 2], 16)
                for a in range(TT):
                    for c in range(2):
                        w0 = D * (kt % 2) + 512 * c
                        last = mm(bank[2 * a + c][:, :], mixT[:, kt, P * a:P * (a + 1)],
                                  dn_ring[:, kt // 2, w0:w0 + 512], start=(kt == 0), stop=(kt == KT - 1))
                last.then_inc(oproj_done, 1)

            fill = {9: 0, 10: 1, 11: 2, 12: 3, 13: 4, 15: 5}
            for g in range(2 * NH):
                if g != NH:
                    score(g)
                if g >= 1:
                    turn_probs(g - 1)
                if g >= 4 and g % 2 == 0:
                    turn_mix((g - 4) // 2)
                if g < NH:
                    project(2, g)
                elif g in fill:
                    out_project(fill[g])
                if g >= 1:
                    pv(g - 1)
                if g == NH:
                    score(g)
            turn_probs(2 * NH - 1)
            turn_mix(NH - 2)
            pv(2 * NH - 1)
            out_project(6)
            turn_mix(NH - 1)
            out_project(7)

            for a in range(TT):
                pe.wait_ge(h2_ready, a + 1)
                for k in range(KT):
                    c = T * (k % 2) + P * a
                    turn(bank[4 + k // 2][:, c:c + P], hmix[:, a, P * k:P * (k + 1)]).then_inc(h2T_done, 1)
            pe.wait_ge(rw_in, 16)
            for k in range(KT):
                if k % 2 == 0:
                    pe.wait_ge(h2T_ready, k // 2 + 1)
                for a in range(TT):
                    last = mm(bank[a][:, 0:NE], h2T[:, k, P * a:P * (a + 1)], rw[:, k, :],
                              start=(k == 0), stop=(k == KT - 1))
            last.then_inc(logits_done, 1)
            pe.wait_ge(tri_made, 1)
            pe.wait_ge(chosen_ready, 1)
            mm(bank[2][:, 0:NE], tri, chosen[:, 0, :], start=True, stop=True)
            mm(bank[2][:, NE:2 * NE], ones, chosen[:, 0, :], start=True, stop=False)
            mm(bank[2][:, NE:2 * NE], tri, chosen[:, 1, :], start=False, stop=True)
            mm(bank[3][:, 0:NE], ones, chosen[:, 0, :], start=True, stop=False)
            mm(bank[3][:, 0:NE], ones, chosen[:, 1, :], start=False, stop=True).then_inc(pos_done, 1)

            def gather(v):
                pe.wait_ge(sel_ready, v)
                for k in range(KT):
                    b, c = 5 + k // 4, P * (k % 4)
                    for a in range(TT):
                        last = mm(bank[b][:, c:c + P], hmix[:, a, P * k:P * (k + 1)],
                                  sel[:, a, :, :].rearrange("p e n -> p (e n)"), start=(a == 0), stop=(a == TT - 1))
                last.then_inc(gather_done, 1)

            def turn_y(v, y):
                pe.wait_ge(selg_ready, v)
                pe.wait_ge(yT_ready, y)
                for a in range(TT):
                    turn(bank[7][:, P * a:P * (a + 1)], selg[:, a, :, :].rearrange("p e n -> p (e n)"))
                for m in range(KT):
                    last = turn(bank[5 + m // 4][:, P * (m % 4):P * (m % 4 + 1)], yT[:, m, :])
                last.then_inc(yT_turned, 1)

            def combine(a, v):
                pe.wait_ge(comb_added, v)
                for c in range(2):
                    last = mm(bank[c][:, :], combT[:, P * a:P * (a + 1)], yrow[:, 512 * c:512 * (c + 1)],
                              start=True, stop=True)
                last.then_inc(comb_done, 1)

            def gate_up(j, half):
                for k in range(KT):
                    s = 8 * half + k
                    pe.wait_ge(gu_in[s], j * 16 + 16)
                    for m in range(2 * KT):
                        last = mm(bank[2 + m // KT][:, CAP * (m % KT):CAP * (m % KT + 1)],
                                  gu_ring[:, s, P * m:P * (m + 1)], xg[:, k, CAP * half:CAP * (half + 1)],
                                  start=(k == 0 and m % KT == 0), stop=(k == KT - 1), skip_group_check=True)
                    last.then_inc(gu_used, 1)

            def down(j, half):
                pe.wait_ge(act_ready, j * 2 + (half + 1))
                pe.wait_ge(yT_ready, j * 2 + (half + 1))
                for k in range(KT):
                    q = k // 2
                    if k % 2 == 0:
                        pe.wait_ge(dn_in[q], j * 32 + 16 * (half + 1))
                    for m in range(KT):
                        w0 = D * (k % 2) + P * m
                        last = mm(bank[4][:, CAP * m:CAP * (m + 1)], dn_ring[:, q, w0:w0 + P], act_t[:, k, :],
                                  start=(k == 0 and m == 0), stop=(k == KT - 1), skip_group_check=True)
                    if k % 2:
                        last.then_inc(dn_used, 1)

            gather(1)
            pe.wait_ge(rounds_ready, 1)
            n = pe.value_load(rounds[0:1, 0:1], min_val=1, max_val=ROUNDS)
            with pe.Fori(0, n) as r:
                with pe.Fori(0, PAIRS) as i:
                    j = r * PAIRS + i
                    pe.wait_ge(xg_ready, j + 1)
                    gate_up(j, 0)
                    turn_y(j + 1, j * 2 + 1)
                    down(j, 0)
                    pe.wait_ge(yrow_ready, j + 1)
                    combine(0, j * 2 + 1)
                    gate_up(j, 1)
                    combine(1, j * 2 + 2)
                    gather(j + 2)
                    down(j, 1)
            turn_y(n * PAIRS + 1, n * (2 * PAIRS) + 1)
            pe.wait_ge(yrow_ready, n * PAIRS + 1)
            combine(0, n * (2 * PAIRS) + 1)
            combine(1, n * (2 * PAIRS) + 2)

        @block.vector
        def _(dve):
            V = nc.vector
            count = [0]

            def link(ins):
                count[0] += 1
                ins.then_inc(dve_step, 1)
                dve.wait_ge(dve_step, count[0])

            V.memset(st[:, 62:63], -0.5).then_inc(consts, 1)
            dve.wait_ge(tables, 5)
            link(V.tensor_scalar(mod_int, dist_int, 3, None, ALU.bitwise_and))
            link(V.tensor_scalar(dist_dil, mod_int, 0.0, None, ALU.is_equal))
            link(V.scalar_tensor_tensor(out=mult, in0=dist_diff, scalar=128.0, in1=dist_dil, op0=ALU.is_le, op1=ALU.add))
            link(V.tensor_scalar(mod_int, dist_int, 15, None, ALU.bitwise_and))
            link(V.tensor_scalar(dist_dil, mod_int, 0.0, None, ALU.is_equal))
            link(V.tensor_tensor(mult, mult, dist_dil, ALU.add))
            link(V.scalar_tensor_tensor(out=mult, in0=dist_diff, scalar=0.0, in1=mult, op0=ALU.is_ge, op1=ALU.mult))
            link(V.tensor_scalar(dist_dil, mult, 0.0, FAR, ALU.is_equal, ALU.mult))
            link(V.tensor_tensor(dist_dil, dist_dil, dist_diff, ALU.max))

            def norm_stats(src, junk, rs_count):
                for a in range(TT):
                    link(V.tensor_tensor_reduce(out=junk[:, a, :], in0=src[:, a, :], in1=src[:, a, :], scale=1.0,
                                                scalar=0.0, op0=ALU.mult, op1=ALU.add, accum_out=st[:, a:a + 1]))
                V.tensor_scalar(st[:, 0:2], st[:, 0:2], 1.0 / D, EPS, ALU.mult, ALU.add).then_inc(ms_ready, 1)
                dve.wait_ge(rs_ready, rs_count)

            dve.wait_ge(x_in, 16 * TT)
            norm_stats(xres, hmix, 1)
            for a in range(TT):
                V.tensor_scalar(hmix[:, a, :], xres[:, a, :], st[:, 2 + a:3 + a], None, ALU.mult).then_inc(h_ready, 1)

            dve.wait_ge(small_in, 16 * 9)
            for i in range(2):
                ins = V.tensor_tensor_reduce(out=lam_rows[:, 2 * i, :], in0=lam_rows[:, 2 * i, :],
                                             in1=lam_rows[:, 2 * i + 1, :], scale=1.0, scalar=0.0,
                                             op0=ALU.mult, op1=ALU.add, accum_out=st[:, 4 + i:5 + i])
                if i == 0:
                    link(ins)
            ins.then_inc(lam_sum, 1)
            dve.wait_ge(prmT_done, 1)
            link(V.tensor_copy(prm[:, :], bank[0][:, 0:17]))
            V.tensor_scalar(prm[:, 16:17], prm[:, 16:17], 1.0 - LAM_INIT, None, ALU.mult).then_inc(prm_ready, 1)
            dve.wait_ge(prm_ready, 1)
            dve.wait_ge(hT_done, 2 * KT)
            for k in (0, 1, 4, 5):
                last = V.tensor_scalar(hT[:, k, :], bank[4 + k // 2][:, T * (k % 2):T * (k % 2 + 1)], prm[:, k:k + 1],
                                       None, ALU.mult)
            last.then_inc(hT_ready_v, 1)
            dve.wait_ge(biasT_done, 2)
            V.tensor_copy(bguT[:, :, :].rearrange("p m e -> p (m e)"), bank[1][:, :])
            V.tensor_copy(bdT[:, :, :].rearrange("p m e -> p (m e)"), bank[2][:, 0:KT * NE]).then_inc(biasT_read, 1)
            dve.wait_ge(lam_exp, 1)
            link(V.tensor_tensor(st[:, 8:9], st[:, 6:7], st[:, 7:8], ALU.subtract))
            link(V.tensor_scalar(st[:, 8:9], st[:, 8:9], LAM_INIT, None, ALU.add))
            dve.wait_ge(w_in_used, 4)
            for b in range(2):
                last = V.tensor_copy(qkT[:, 4 + 2 * b:6 + 2 * b, :].rearrange("p m t -> p (m t)"), bank[2 + b][:, :])
            last.then_inc(proj_ready_v, 1)
            dve.wait_ge(w_in_used, 8)
            for a in range(TT):
                last = V.tensor_copy(vS[:, a, 0:512], bank[4 + a][:, :])
            last.then_inc(proj_ready_v, 1)

            def negated_scores(g):
                dve.wait_ge(scores_done, g + 1)
                slope = SLOPES[2 * (g % NH) + (g >= NH)]
                dist = dist_diff if g < NH else dist_dil
                maps = 2 if g < NH else 1
                s = scores[g % 2]
                V.scalar_tensor_tensor(out=s[:, 0:maps, :], in0=dist.unsqueeze(1).broadcast_to([P, maps, T + P]),
                                       scalar=slope, in1=psum[:, 4:4 + maps, 0:T + P], op0=ALU.mult,
                                       op1=ALU.subtract).then_inc(scores_read, 1)
                dve.wait_ge(scores_read, g + 1)
                for c, w, i in ((0, T, 2), (T, P, 0)):
                    lo = 24 + 4 * (g % 2) + i
                    ins = V.tensor_reduce(st[:, lo:lo + maps], s[:, 0:maps, c:c + w], AX.X, ALU.min)
                ins.then_inc(max_ready, 1)

            def diff_probs(g):
                dve.wait_ge(exp_done, g + 1)
                s, pr = scores[g % 2], probs[g % 2]
                link(V.reciprocal(st[:, 56:60], st[:, 32 + 4 * (g % 2):36 + 4 * (g % 2)]))
                link(V.tensor_scalar(st[:, 57:60:2], st[:, 57:60:2], st[:, 8:9], None, ALU.mult))
                for c, w, z in ((0, T, 58), (T, P, 56)):
                    p1, p2 = s[:, 0, c:c + w], s[:, 1, c:c + w]
                    link(V.tensor_scalar(p2, p2, st[:, z + 1:z + 2], None, ALU.mult))
                    ins = V.scalar_tensor_tensor(out=pr[:, c:c + w], in0=p1, scalar=st[:, z:z + 1], in1=p2,
                                                 op0=ALU.mult, op1=ALU.subtract)
                ins.then_inc(probs_ready, 1)

            def dil_probs(g):
                dve.wait_ge(exp_done, g + 1)
                dve.wait_ge(probs_ready, g)
                s, pr = scores[g % 2], probs[g % 2]
                if g >= NH + 2:
                    dve.wait_ge(pv_read, g - 1)
                z = 40 + 2 * (g % 2)
                for c, w, a in ((0, T, 1), (T, P, 0)):
                    link(V.scalar_tensor_tensor(out=pr[:, c:c + w], in0=s[:, 0, c:c + w], scalar=1.0,
                                                in1=mult[:, c:c + w], op0=ALU.mult, op1=ALU.mult,
                                                accum_out=st[:, 50 + a:51 + a]))
                V.reciprocal(st[:, z:z + 2], st[:, 50:52]).then_inc(probs_ready, 1)

            def norm_pair(kt):
                dve.wait_ge(pv_read, 2 * kt + 2)
                hv = hmix[:, :, P * kt:P * (kt + 1)]
                sq = posm[:, :, 0:P]
                link(V.tensor_tensor(sq, hv, hv, ALU.mult))
                link(V.tensor_reduce(st[:, 12:16].rearrange("p (a h) -> p a h", a=TT),
                                     sq.rearrange("p a (h d) -> p a h d", d=HD), AX.X, ALU.add))
                V.tensor_scalar(st[:, 16:20], st[:, 12:16], 1.0 / HD, EPS, ALU.mult, ALU.add).then_inc(ms_ready, 1)
                dve.wait_ge(rs_ready, 2 + kt)
                hv4 = hv.rearrange("p a (h d) -> p a h d", d=HD)
                rs = st[:, 20:24].rearrange("p (a h) -> p a h", a=TT).unsqueeze(3).broadcast_to([P, TT, 2, HD])
                V.tensor_tensor(hv4, hv4, rs, ALU.mult).then_inc(mix_ready, 1)

            link(V.tensor_scalar(scores[0][:, 0, :], dist_diff, 0.0, FAR, ALU.is_lt, ALU.mult))
            link(V.tensor_tensor(dist_diff, dist_diff, scores[0][:, 0, :], ALU.max))
            negated_scores(0)
            for g in range(2 * NH):
                if g + 1 < 2 * NH and g + 1 != NH:
                    negated_scores(g + 1)
                if g == NH - 1:
                    dve.wait_ge(w_in_used, 12)
                    for b in range(2):
                        last = V.tensor_copy(qkT[:, 12 + 2 * b:14 + 2 * b, :].rearrange("p m t -> p (m t)"), bank[b][:, :])
                    last.then_inc(proj_ready_v, 1)
                if g < NH:
                    diff_probs(g)
                else:
                    dil_probs(g)
                if g == NH - 1:
                    negated_scores(NH)
                if g >= 2 and g % 2 == 0 and g <= NH:
                    norm_pair((g - 2) // 2)

            dve.wait_ge(oproj_done, KT)
            for a in range(TT):
                for c in range(2):
                    link(V.tensor_tensor(xres[:, a, 512 * c:512 * (c + 1)], xres[:, a, 512 * c:512 * (c + 1)],
                                         bank[2 * a + c][:, :], ALU.add))
            norm_stats(xres, hmix, 2 + NH // 2)
            for a in range(TT):
                V.tensor_scalar(hmix[:, a, :], xres[:, a, :], st[:, 2 + a:3 + a], None, ALU.mult).then_inc(h2_ready, 1)
            dve.wait_ge(h2T_done, 2 * KT)
            ffn_w = prm[:, 8:16]
            for b in range(4):
                V.tensor_tensor(h2T[:, 2 * b:2 * b + 2, :], bank[4 + b][:, :].rearrange("p (k t) -> p k t", k=2),
                                ffn_w[:, 2 * b:2 * b + 2].unsqueeze(2).broadcast_to([P, 2, T]), ALU.mult)\
                    .then_inc(h2T_ready, 1)
            dve.wait_ge(tables, 6)
            link(V.tensor_copy(iota_e, iota[:, 0:NE]))
            dve.wait_ge(logits_done, 1)
            for a in range(TT):
                link(V.tensor_tensor(logits[:, a, :], bank[a][:, 0:NE], rb[:, :], ALU.add))
            for a in range(TT):
                link(V.max(top_v[:, a, :], logits[:, a, :]))
            V.tensor_scalar(st[:, 46:48], top_v[:, :, 0], -1.0, None, ALU.mult).then_inc(top_ready, 1)
            for a in range(TT):
                link(V.max_index(top_i[:, a, :], top_v[:, a, :], logits[:, a, :]))
            link(V.tensor_copy(top_f, top_i))
            wide = [P, TT, TOPK, NE]
            link(V.tensor_tensor(sel_k, iota_e.unsqueeze(1).unsqueeze(1).broadcast_to(wide),
                                 top_f[:, :, 0:TOPK].unsqueeze(3).broadcast_to(wide), ALU.is_equal))
            V.tensor_reduce(chosen, sel_k.rearrange("p a k e -> p a e k"), AX.X, ALU.add).then_inc(chosen_ready, 1)
            dve.wait_ge(top_exp, 1)
            link(V.reciprocal(st[:, 52:54], st[:, 48:50]))
            link(V.tensor_tensor(top_e[:, :, 0:TOPK], top_e[:, :, 0:TOPK],
                                 st[:, 52:54].unsqueeze(2).broadcast_to([P, TT, TOPK]), ALU.mult))
            link(V.tensor_tensor(selg_k, sel_k, top_e[:, :, 0:TOPK].unsqueeze(3).broadcast_to(wide), ALU.mult))
            link(V.tensor_reduce(gates[:, :, 2:2 + NE], selg_k.rearrange("p a k e -> p a e k"), AX.X, ALU.add))
            link(V.tensor_copy(gates[:, :, 0:2], gates[:, :, NE:NE + 2]))
            dve.wait_ge(pos_done, 1)
            link(V.memset(posm[:, :, :], -1.0))
            link(V.scalar_tensor_tensor(out=slot0, in0=bank[2][:, 0:2 * NE].rearrange("p (a e) -> p a e", a=TT),
                                        scalar=1.0, in1=chosen, op0=ALU.add, op1=ALU.mult))
            for r in range(ROUNDS):
                link(V.tensor_scalar(posm[:, :, 2 + NE * r:2 + NE * (r + 1)], slot0, 1.0 + CAP * r, None, ALU.subtract))
            link(V.reduce_max(st[:, 54:55], bank[3][:, 0:NE], AX.X))
            link(V.tensor_scalar(st[:, 55:56], st[:, 54:55], float(CAP), 1.0, ALU.is_gt, ALU.add))
            for r in range(2, ROUNDS):
                link(V.scalar_tensor_tensor(out=st[:, 55:56], in0=st[:, 54:55], scalar=float(CAP * r), in1=st[:, 55:56],
                                            op0=ALU.is_gt, op1=ALU.add))
            V.tensor_copy(rounds[:, :], st[:, 55:56]).then_inc(rounds_ready, 1)
            V.memset(yT, 0.0).then_inc(yT_ready, 1)
            V.memset(st[:, 60:61], 0.0).then_inc(comb_added, 1)

            four = [P, TT, 2, CAP]

            def one_hot(dst, c):
                return V.tensor_tensor(dst, posm[:, :, bass.ds(c, 2)].unsqueeze(3).broadcast_to(four),
                                       iota[:, :].unsqueeze(1).unsqueeze(1).broadcast_to(four), ALU.is_equal)

            def keep_xg(v):
                dve.wait_ge(gather_done, v)
                V.tensor_tensor(xg, psum[:, 5:7, :].rearrange("p b (k n) -> p (b k) n", k=4),
                                ffn_w.unsqueeze(2).broadcast_to([P, KT, P]), ALU.mult).then_inc(xg_ready, 1)

            one_hot(sel, 2).then_inc(sel_ready, 1)
            keep_xg(1)
            dve.wait_ge(rounds_ready, 1)
            n = dve.value_load(rounds[0:1, 0:1], min_val=1, max_val=ROUNDS)

            STEPS = 9

            def body(j, i, chain):
                dve.wait_ge(gather_done, j + 1)
                chain(one_hot(selg, j * 2))
                V.tensor_tensor(selg, selg, gates[:, :, bass.ds(i * 2, 2)].unsqueeze(3).broadcast_to(four),
                                ALU.mult).then_inc(selg_ready, 1)

            def add_combined(a, v):
                dve.wait_ge(comb_done, v)
                xs = xres[:, a, :].rearrange("p (c n) -> p c n", c=2)
                V.tensor_tensor(xs, xs, psum[:, 0:2, :], ALU.add).then_inc(comb_added, 1)

            def expert(j, i, half, chain):
                e = i * 2 + half
                eight = [P, KT, CAP]
                gate_b = bguT[:, 0:KT, bass.ds(e, 1)].broadcast_to(eight)
                up_b = bguT[:, KT:2 * KT, bass.ds(e, 1)].broadcast_to(eight)
                dve.wait_ge(gu_used, j * GUN + 8 * (half + 1))
                chain(V.tensor_tensor(gate_t, bank[2][:, :].rearrange("p (m n) -> p m n", m=KT), gate_b, ALU.add))
                V.tensor_scalar(gate_t, gate_t, LIMIT, None, ALU.min).then_inc(gate_ready, 1)
                chain(V.tensor_tensor(up_t, bank[3][:, :].rearrange("p (m n) -> p m n", m=KT), up_b, ALU.add))
                chain(V.tensor_scalar(up_t, up_t, -LIMIT, LIMIT, ALU.max, ALU.min))
                dve.wait_ge(gate_ready, j * 2 + (half + 1))
                flat = "p m n -> p (m n)"
                chain(V.scalar_tensor_tensor(out=up_t.rearrange(flat), in0=up_t.rearrange(flat), scalar=1.0,
                                             in1=gate_t.rearrange(flat), op0=ALU.add, op1=ALU.mult))
                dve.wait_ge(sig_ready, j * 2 + (half + 1))
                V.tensor_tensor(act_t, up_t, sig_t, ALU.mult).then_inc(act_ready, 1)

            def keep_y(j, i, half):
                dve.wait_ge(dn_used, j * (2 * DNN) + DNN * (half + 1))
                V.tensor_tensor(yT[:, :, CAP * half:CAP * (half + 1)], bank[4][:, :].rearrange("p (m n) -> p m n", m=KT),
                                bdT[:, :, bass.ds(i * 2 + half, 1)].broadcast_to([P, KT, CAP]), ALU.add)\
                    .then_inc(yT_ready, 1)

            with dve.Fori(0, n) as r:
                with dve.Fori(0, PAIRS) as i:
                    j = r * PAIRS + i
                    at = [0]

                    def chain(ins):
                        at[0] += 1
                        ins.then_inc(dve_loop, 1)
                        dve.wait_ge(dve_loop, j * STEPS + at[0])

                    body(j, i, chain)
                    one_hot(sel, j * 2 + 4).then_inc(sel_ready, 1)
                    expert(j, i, 0, chain)
                    keep_y(j, i, 0)
                    add_combined(0, j * 2 + 1)
                    expert(j, i, 1, chain)
                    add_combined(1, j * 2 + 2)
                    keep_xg(j + 2)
                    keep_y(j, i, 1)
                    assert at[0] == STEPS, at[0]
            last_j = n * PAIRS

            def chain(ins):
                ins.then_inc(dve_loop, 1)
                dve.wait_ge(dve_loop, last_j * STEPS + 1)

            body(last_j, PAIRS, chain)
            add_combined(0, last_j * 2 + 1)
            add_combined(1, last_j * 2 + 2)
            dve.wait_ge(comb_added, last_j * 2 + 3)

            norm_stats(xres, hmix, 3 + NH // 2)
            dve.wait_ge(fw_in, 16)
            for a in range(TT):
                V.scalar_tensor_tensor(out=hmix[:, a, :], in0=xres[:, a, :], scalar=st[:, 2 + a:3 + a],
                                       in1=gu_ring[:, 0, 0:D], op0=ALU.mult, op1=ALU.mult).then_inc(h_ready, 1)


_INS = ['x', 'attn_norm_w', 'w_in', 'diff_lambda_q1', 'diff_lambda_k1', 'diff_lambda_q2', 'diff_lambda_k2',
        'diff_subln_w', 'w_out', 'ffn_norm_w', 'router_w', 'router_b', 'w_gate_up', 'b_gate_up', 'w_down', 'b_down',
        'final_norm_w']


def kernel(**inputs):
    import concourse.bacc as _bacc
    from concourse.bass_utils import run_bass_kernel_spmd as _run

    nc = _bacc.Bacc("TRN2", target_bir_lowering=False, num_devices=1)
    arrays, args = {}, []
    for name in _INS:
        a = np.ascontiguousarray(inputs[name])
        arrays[f"in_{name}_dram"] = a
        args.append(nc.dram_tensor(f"in_{name}_dram", a.shape, mybir.dt.from_np(a.dtype), kind="ExternalInput").ap())
    out = nc.dram_tensor("out_0_dram", (1, T, D), F32, kind="ExternalOutput").ap()
    moe_block(nc, *args, out)
    r = _run(nc, [arrays], core_ids=[0])
    return r.results[0]["out_0_dram"]
```

```python
import numpy as np
import concourse.bass as bass
from concourse import mybir
from concourse.alu_op_type import AluOpType as ALU
from contextlib import ExitStack

F32 = mybir.dt.float32
I32 = mybir.dt.int32
U32 = mybir.dt.uint32
BF16 = mybir.dt.bfloat16
ACT = mybir.ActivationFunctionType
AX = mybir.AxisListType

P = 128
T, D = 256, 1024
TT = T // P
KT = D // P
HD = 64
NH = 8
DK = HD // 2
EPS = 1e-5
LAM_INIT = 0.8 - 0.6
NE, TOPK, FF = 32, 4, 1024
LIMIT, ALPHA = 7.0, 1.702
CAP = 64
PAIRS = NE // 2
ROUNDS = T // CAP
SLOPES = [2.0 ** (-8.0 * (i + 1) / (2 * NH)) for i in range(2 * NH)]
FAR = 1e30
WS = 2048
GUN, DNN = 16, 4


def moe_block(nc, x, attn_norm_w, w_in, lq1, lk1, lq2, lk2, subln_w, w_out, ffn_norm_w, router_w, router_b,
              w_gate_up, b_gate_up, w_down, b_down, final_norm_w, out):
    ctx = ExitStack()
    with ctx:
        def sb(name, shape, dt=F32):
            return ctx.enter_context(nc.sbuf_tensor(name, shape, dt))

        def sem(name):
            return ctx.enter_context(nc.semaphore(name))

        gu_ring = sb("gu_ring", [P, GUN, WS])
        dn_ring = sb("dn_ring", [P, DNN, WS])
        xres = sb("xres", [P, TT, D])
        hmix = sb("hmix", [P, TT, D])
        shared = sb("shared", [P, 7424])
        posm = sb("posm", [P, TT, 2 + NE * ROUNDS + 2])
        gates = sb("gates", [P, TT, 2 + NE])
        ident = sb("ident", [P, P])
        iota = sb("iota", [P, CAP])
        prm = sb("prm", [P, 17])
        rb = sb("rb", [P, NE])
        st = sb("st", [P, 64])
        rounds = sb("rounds", [P, 1], I32)
        more_rounds = sb("more_rounds", [P, 1], I32)

        hT = gu_ring[:, 12, :].rearrange("p (k t) -> p k t", k=KT)
        qkT = gu_ring[:, 13:15, :].rearrange("p s (m t) -> p (s m) t", t=T)
        vS = gu_ring[:, 15, :].rearrange("p (a c) -> p a c", a=TT)
        NB = 2 * FF + D
        dn_flat = dn_ring[:, :, :].rearrange("p s c -> p (s c)")
        bias_rows, bias_rest = dn_flat[:, 0:NB], dn_flat[:, 2 * WS:2 * WS + NB]

        def part(a, n):
            return shared[:, a:a + n]

        mixT = part(0, 2048).rearrange("p (k t) -> p k t", k=KT)
        h2T = mixT
        scores = [part(2048 + 768 * i, 768).rearrange("p (m j) -> p m j", m=2) for i in range(2)]
        probs = [part(3584 + 384 * i, 384) for i in range(2)]
        probsT = part(4352, 384)
        dist_diff = part(4736, 384)
        dist_dil = part(5120, 384)
        mult = part(5504, 384)
        bias3 = part(5888, NB // 2).bitcast(BF16)
        rw = part(5120, 256).rearrange("p (k e) -> p k e", k=KT)
        tri = part(4736, P)
        ones = part(4736 + P, P)
        lam_rows = part(2048, 4 * DK).rearrange("p (v d) -> p v d", v=4)
        prm_rows = part(3584, P)[0:17, :]
        dist_int = part(4352, 384).bitcast(I32)
        mod_int = part(3584 + P, 384).bitcast(I32)
        sel_k = part(2048, 256).rearrange("p (a k e) -> p a k e", a=TT, k=TOPK)
        selg_k = part(2304, 256).rearrange("p (a k e) -> p a k e", a=TT, k=TOPK)
        chosen = part(2560, TT * NE).rearrange("p (a e) -> p a e", a=TT)
        logits = part(2624, TT * NE).rearrange("p (a e) -> p a e", a=TT)
        slot0 = part(2688, TT * NE).rearrange("p (a e) -> p a e", a=TT)
        logitsT = part(3072, T)
        iota_e = part(2752, NE)
        top_v = part(2784, 16).rearrange("p (a k) -> p a k", a=TT)
        top_i = part(2800, 16).bitcast(U32).rearrange("p (a k) -> p a k", a=TT)
        top_f = part(2816, 16).rearrange("p (a k) -> p a k", a=TT)
        top_e = part(2832, 16).rearrange("p (a k) -> p a k", a=TT)

        xg = part(0, 1024).rearrange("p (k n) -> p k n", k=KT)
        gate_t = part(1024, 512)
        up_t = part(1536, 512)
        sig_t = part(2048, 512)
        act_t = part(2560, 512)
        actT = part(3072, 512)
        yrow = part(3584, 512)
        combT = part(4096, 256)
        sel = part(4352, 256).rearrange("p (a e n) -> p a e n", a=TT, e=2)
        selg = part(4608, 256).rearrange("p (a e n) -> p a e n", a=TT, e=2)
        bias_sel = part(4992, CAP // 2).bitcast(BF16)
        expert_of = part(5024, NE + 1)

        psum = ctx.enter_context(nc.psum_tensor("psum", [P, 8, 512], F32))
        bank = [psum[:, i, :] for i in range(8)]

        x_in = sem("x_in")
        prm_in = sem("prm_in")
        small_in = sem("small_in")
        bias_in = sem("bias_in")
        rw_in = sem("rw_in")
        w_in_in = [sem(f"w_in_in{i}") for i in range(12)]
        w_out_in = [sem(f"w_out_in{i}") for i in range(4)]
        gu_in = [sem(f"gu_in{i}") for i in range(GUN)]
        dn_in = [sem(f"dn_in{i}") for i in range(DNN)]
        fw_in = sem("fw_in")
        out_done = sem("out_done")
        pool_step = sem("pool_step")
        tables = sem("tables")
        tri_made = sem("tri_made")
        dve_step = sem("dve_step")
        sq_done = sem("sq_done")
        x1_done = sem("x1_done")
        x1_ready = sem("x1_ready")
        ms_ready = sem("ms_ready")
        rs_ready = sem("rs_ready")
        consts = sem("consts")
        h_ready = sem("h_ready")
        prmT_done = sem("prmT_done")
        prm_ready = sem("prm_ready")
        bias_split = sem("bias_split")
        hT_done = sem("hT_done")
        hT_ready_v = sem("hT_ready_v")
        hT_ready_a = sem("hT_ready_a")
        w_in_used = sem("w_in_used")
        proj_ready_v = sem("proj_ready_v")
        proj_ready_a = sem("proj_ready_a")
        lam_sum = sem("lam_sum")
        lam_exp = sem("lam_exp")
        scores_done = sem("scores_done")
        scores_read = sem("scores_read")
        max_ready = sem("max_ready")
        exp_done = sem("exp_done")
        probs_ready = sem("probs_ready")
        probsT_done = sem("probsT_done")
        probsT_ready = sem("probsT_ready")
        pv_done = sem("pv_done")
        pv_read = sem("pv_read")
        mix_ready = sem("mix_ready")
        mixT_done = sem("mixT_done")
        mixT_ready = sem("mixT_ready")
        oproj_done = sem("oproj_done")
        h2_ready = sem("h2_ready")
        h2T_done = sem("h2T_done")
        h2T_ready_v = sem("h2T_ready_v")
        h2T_ready_a = sem("h2T_ready_a")
        logitsT_done = sem("logitsT_done")
        logitsT_ready = sem("logitsT_ready")
        logits_done = sem("logits_done")
        top_ready = sem("top_ready")
        top_exp = sem("top_exp")
        chosen_ready = sem("chosen_ready")
        pos_done = sem("pos_done")
        rounds_ready = sem("rounds_ready")
        sel_ready = sem("sel_ready")
        selg_ready = sem("selg_ready")
        gather_done = sem("gather_done")
        xg_ready = sem("xg_ready")
        gu_used = sem("gu_used")
        dn_used = sem("dn_used")
        gate_ready = sem("gate_ready")
        sig_ready = sem("sig_ready")
        act_ready = sem("act_ready")
        bias_sel_ready = sem("bias_sel_ready")
        selT_done = sem("selT_done")
        combT_ready = sem("combT_ready")
        actT_done = sem("actT_done")
        actT_ready = sem("actT_ready")
        yrow_ready = sem("yrow_ready")
        comb_done = sem("comb_done")
        comb_added = sem("comb_added")
        dve_loop = sem("dve_loop")
        lin_ready = sem("lin_ready")

        tok = "b (a p) d -> p (b a) d"
        GROUP_C_AT = {0: (0, 1), 1: (2,), 2: (3,), 3: (4,), 4: (5,), 5: (6,), 6: (7,)}
        TURN_AT = {4: 0, 6: 1, 8: 2, 10: 3, 11: 4, 13: 5, 15: 6}
        OUT_AT = {7: 0, 8: 1, 9: 2, 11: 3, 12: 4, 14: 5}
        block = ctx.enter_context(nc.Block())

        @block.sync
        def _(sp):
            xv = x.rearrange(tok, p=P)
            for a in range(TT):
                sp.dma_start(xres[:, a, :], xv[:, a, :]).then_inc(x_in, 16)
            sp.dma_start(prm_rows[0:8, :], attn_norm_w.rearrange("o (k p) -> (o k) p", p=P)).then_inc(prm_in, 16)
            sp.dma_start(prm_rows[8:16, :], ffn_norm_w.rearrange("o (k p) -> (o k) p", p=P)).then_inc(prm_in, 16)
            for i in range(2):
                sp.dma_start(prm_rows[16:17, HD * i:HD * (i + 1)], subln_w).then_inc(prm_in, 16)
            w_in_v = w_in.rearrange("o (k p) c -> p (o k) c", p=P)
            for g in range(3):
                for q in range(4):
                    s = 4 * g + q
                    sp.dma_start(gu_ring[:, s, :].rearrange("p (k c) -> p k c", k=2),
                                 w_in_v[:, 2 * q:2 * q + 2, D * g:D * (g + 1)]).then_inc(w_in_in[s], 16)
            w_out_v = w_out.rearrange("o (k p) c -> p (o k) c", p=P)
            sp.wait_ge(bias_split, 1)
            for q in range(4):
                sp.dma_start(dn_ring[:, q, :].rearrange("p (k c) -> p k c", k=2),
                             w_out_v[:, 2 * q:2 * q + 2, :]).then_inc(w_out_in[q], 16)

            gu_v = w_gate_up[0, :, :, :].rearrange("e (k p) c -> p e k c", p=P)
            dn_v = w_down[0, :, :, :].rearrange("e (k p) c -> p e k c", p=P)

            def load_gu(e, half, k):
                s = 8 * half + k
                sp.dma_start(gu_ring[:, s, :].rearrange("p (e c) -> p e c", e=1),
                             gu_v[:, bass.ds(e, 1), k, :]).then_inc(gu_in[s], 16)

            def load_dn(e, q):
                sp.dma_start(dn_ring[:, q:q + 1, :].rearrange("p e (k c) -> p e k c", k=2),
                             dn_v[:, bass.ds(e, 1), 2 * q:2 * q + 2, :]).then_inc(dn_in[q], 16)

            for s in range(GUN):
                if s < 12:
                    sp.wait_ge(w_in_used, s + 1)
                elif s == 12:
                    sp.wait_ge(w_in_used, 12)
                elif s < 15:
                    sp.wait_ge(scores_done, 2 * NH)
                else:
                    sp.wait_ge(pv_done, 2 * NH)
                load_gu(s // 8, s // 8, s % 8)
            for q in range(DNN):
                if q < DNN - 1:
                    sp.wait_ge(oproj_done, 2 * q + 2)
                else:
                    sp.wait_ge(x1_done, TT)
                load_dn(0, q)
            sp.wait_ge(rounds_ready, 2)
            more = sp.value_load(more_rounds[0:1, 0:1], min_val=0, max_val=ROUNDS - 1)

            def load_gu_half(j, e, half):
                for k in range(KT):
                    sp.wait_ge(gu_used, j * GUN + (8 * half + k + 1))
                    load_gu(e + half, half, k)

            def load_dn_first(j, e):
                for q in range(DNN):
                    sp.wait_ge(dn_used, j * (2 * DNN) + (DNN + q + 1))
                    load_dn(e, q)

            def load_dn_second(j, e):
                for q in range(DNN):
                    sp.wait_ge(dn_used, j * (2 * DNN) + (q + 1))
                    load_dn(e, q)

            for j in range(2):
                load_gu_half(j, 2 * j + 2, 0)
                load_dn_second(j, 2 * j + 1)
                load_gu_half(j, 2 * j + 2, 1)
                load_dn_first(j, 2 * j + 2)
            with sp.Fori(2, more * PAIRS + (PAIRS - 2)) as j:
                e = ((j + 1) % PAIRS) * 2
                load_gu_half(j, e, 0)
                load_dn_second(j, (j % PAIRS) * 2 + 1)
                load_dn_first(j, e)
                load_gu_half(j, e, 1)
            j = more * PAIRS + (PAIRS - 2)
            load_dn_second(j, NE - 3)
            load_gu_half(j, NE - 2, 0)
            load_dn_first(j, NE - 2)
            load_gu_half(j, NE - 2, 1)
            load_dn_second(more * PAIRS + (PAIRS - 1), NE - 1)
            sp.wait_ge(gu_used, more * (PAIRS * GUN) + PAIRS * GUN)
            sp.dma_start(gu_ring[:, 0, 0:D], final_norm_w.rearrange("(a d) -> a d", a=1).broadcast_to([P, D]))\
                .then_inc(fw_in, 16)
            out_v = out.rearrange(tok, p=P)
            for a in range(TT):
                sp.wait_ge(h_ready, TT + a + 1)
                sp.dma_start(out_v[:, a, :], hmix[:, a, :]).then_inc(out_done, 16)
            sp.wait_ge(out_done, 16 * TT)

        @block.gpsimd
        def _(pool):
            count = [0]

            def link(ins):
                count[0] += 1
                ins.then_inc(pool_step, 1)
                pool.wait_ge(pool_step, count[0])

            def eye(m):
                link(nc.gpsimd.memset(m, 0.0))
                return nc.gpsimd.affine_select(out=m, in_=m, compare_op=ALU.not_equal, fill=1.0, base=0,
                                               pattern=[[-1, P]], channel_multiplier=1)

            eye(ident[:, :]).then_inc(tables, 1)
            for dst in (dist_diff, dist_int):
                nc.gpsimd.iota(dst[:, T:T + P], pattern=[[-1, P]], base=0, channel_multiplier=1,
                               allow_small_or_imprecise_dtypes=True).then_inc(tables, 1)
                nc.gpsimd.iota(dst[:, 0:T], pattern=[[-1, T]], base=P, channel_multiplier=1,
                               allow_small_or_imprecise_dtypes=True).then_inc(tables, 1)
            nc.gpsimd.iota(iota[:, :], pattern=[[1, CAP]], base=0, channel_multiplier=0,
                           allow_small_or_imprecise_dtypes=True).then_inc(tables, 1)

            def rsqrt(n, src, dst):
                pool.wait_ge(ms_ready, n)
                nc.gpsimd.tensor_tensor(dst, src, st[:, 62:63].broadcast_to(list(dst.shape)), ALU.pow)\
                    .then_inc(rs_ready, 1)

            pool.wait_ge(consts, 1)
            rsqrt(1, st[:, 0:2], st[:, 2:4])
            for i in range(NH // 2):
                rsqrt(2 + i, st[:, 16:20], st[:, 20:24])
            pool.wait_ge(probs_ready, 2 * NH)
            link(nc.gpsimd.memset(ones, 1.0))
            nc.gpsimd.affine_select(out=tri, in_=ones, compare_op=ALU.is_gt, fill=0.0, base=0,
                                    pattern=[[1, P]], channel_multiplier=-1).then_inc(tri_made, 1)
            rsqrt(2 + NH // 2, st[:, 0:2], st[:, 2:4])
            for a in range(TT):
                rsqrt(3 + NH // 2 + a, st[:, a:a + 1], st[:, 2 + a:3 + a])

        @block.scalar
        def _(act):
            for i, v in enumerate((lq1, lk1, lq2, lk2)):
                act.dma_start(lam_rows[:, i, :], v.broadcast_to([P, DK])).then_inc(small_in, 16)
            act.dma_start(rb[:, :], router_b.broadcast_to([P, NE])).then_inc(small_in, 16)
            for q in range(3):
                rows = bias_rows[NE * q:NE * (q + 1), :]
                act.dma_start(rows[:, 0:2 * FF], b_gate_up[0, :, :]).then_inc(bias_in, 16)
                act.dma_start(rows[:, 2 * FF:NB], b_down[0, :, :]).then_inc(bias_in, 16)

            def squares(a):
                return nc.scalar.activation(hmix[:, a, :], xres[:, a, :], ACT.Square, accum_out=st[:, a:a + 1])

            act.wait_ge(x_in, 16 * TT)
            squares(0)
            squares(1).then_inc(sq_done, 1)
            act.wait_ge(prm_ready, 1)
            act.wait_ge(hT_done, 2 * KT)
            for k in (2, 3, 6, 7):
                last = nc.scalar.activation(hT[:, k, :], bank[4 + k // 2][:, T * (k % 2):T * (k % 2 + 1)], ACT.Copy,
                                            scale=prm[:, k:k + 1])
            last.then_inc(hT_ready_a, 1)
            act.wait_ge(w_in_used, 4)
            for b in range(2):
                last = nc.scalar.activation(qkT[:, 2 * b:2 * b + 2, :].rearrange("p m t -> p (m t)"), bank[b][:, :],
                                            ACT.Copy, scale=DK ** -0.5)
            last.then_inc(proj_ready_a, 1)
            act.wait_ge(lam_sum, 1)
            nc.scalar.activation(st[:, 6:8], st[:, 4:6], ACT.Exp).then_inc(lam_exp, 1)
            act.wait_ge(w_in_used, 8)
            for b in range(2):
                last = nc.scalar.activation(qkT[:, 8 + 2 * b:10 + 2 * b, :].rearrange("p m t -> p (m t)"),
                                            bank[6 + b][:, :], ACT.Copy, scale=HD ** -0.5)
            last.then_inc(proj_ready_a, 1)

            def exps(g):
                act.wait_ge(max_ready, g + 1)
                s = scores[g % 2]
                lo, z = 24 + 4 * (g % 2), 32 + 4 * (g % 2)
                maps = 2 if g < NH else 1
                for c, w, i in ((0, T, 2), (T, P, 0)):
                    for m in range(maps):
                        acc = {"accum_out": st[:, z + i + m:z + i + m + 1]} if g < NH else {}
                        last = nc.scalar.activation(s[:, m, c:c + w], s[:, m, c:c + w], ACT.Exp,
                                                    bias=st[:, lo + i + m:lo + i + m + 1], scale=-1.0, **acc)
                last.then_inc(exp_done, 1)

            def turn_probs(g):
                act.wait_ge(probsT_done, g + 1)
                if g >= 1:
                    act.wait_ge(pv_done, g)
                nc.scalar.activation(probsT, bank[6][:, 0:384], ACT.Copy).then_inc(probsT_ready, 1)

            def keep_pv(g):
                act.wait_ge(pv_done, g + 1)
                if g < NH:
                    nc.scalar.activation(hmix[:, :, HD * g:HD * (g + 1)],
                                         bank[7][:, 0:P].rearrange("p (a d) -> p a d", a=TT), ACT.Copy)\
                        .then_inc(pv_read, 1)
                else:
                    for a in range(TT):
                        last = nc.scalar.activation(hmix[:, a, HD * g:HD * (g + 1)], bank[7][:, HD * a:HD * (a + 1)],
                                                    ACT.Copy, scale=st[:, 40 + 2 * (g % 2) + a:41 + 2 * (g % 2) + a])
                    last.then_inc(pv_read, 1)

            def keep_mixT(kt):
                act.wait_ge(mixT_done, kt + 1)
                scale = prm[:, 16:17] if kt < NH // 2 else 1.0
                nc.scalar.activation(mixT[:, kt, :], bank[7][:, P:P + T], ACT.Copy, scale=scale)\
                    .then_inc(mixT_ready, 1)

            exps(0)
            for g in range(2 * NH + 1):
                if g >= 1:
                    turn_probs(g - 1)
                if g == NH - 1:
                    act.wait_ge(w_in_used, 12)
                    for a in range(TT):
                        last = nc.scalar.activation(vS[:, a, 512:D], bank[2 + a][:, :], ACT.Copy)
                    last.then_inc(proj_ready_a, 1)
                if g + 1 < 2 * NH:
                    exps(g + 1)
                if g in TURN_AT:
                    keep_mixT(TURN_AT[g])
                if g >= 1:
                    keep_pv(g - 1)
            act.dma_start(rw, router_w.rearrange("o (k p) e -> p (o k) e", p=P)).then_inc(rw_in, 16)
            keep_mixT(NH - 1)

            act.wait_ge(x1_ready, 1)
            squares(0)
            act.wait_ge(x1_ready, 2)
            squares(1).then_inc(sq_done, 1)
            act.wait_ge(h2T_done, 2 * KT)
            for b in (1, 3):
                for k in (2 * b, 2 * b + 1):
                    last = nc.scalar.activation(h2T[:, k, :], bank[4 + b][:, T * (k % 2):T * (k % 2 + 1)], ACT.Copy,
                                                scale=prm[:, 8 + k:9 + k])
                last.then_inc(h2T_ready_a, 1)

            act.wait_ge(top_ready, 1)
            for a in range(TT):
                last = nc.scalar.activation(top_e[:, a, 0:TOPK], top_v[:, a, 0:TOPK], ACT.Exp, bias=st[:, 46 + a:47 + a],
                                            accum_out=st[:, 48 + a:49 + a])
            last.then_inc(top_exp, 1)

            act.wait_ge(rounds_ready, 1)
            n = act.value_load(rounds[0:1, 0:1], min_val=1, max_val=ROUNDS)

            def keep_combT(v):
                act.wait_ge(selT_done, v)
                nc.scalar.activation(combT, bank[7][:, 0:T], ACT.Copy).then_inc(combT_ready, 1)

            def expert(j, half):
                keep_combT(j * 2 + (half + 1))
                act.wait_ge(gate_ready, j * 2 + (half + 1))
                nc.scalar.activation(sig_t, gate_t, ACT.Sigmoid, scale=ALPHA).then_inc(sig_ready, 1)
                act.wait_ge(actT_done, j * 2 + (half + 1))
                nc.scalar.activation(actT, bank[7][:, :], ACT.Copy).then_inc(actT_ready, 1)
                act.wait_ge(dn_used, j * (2 * DNN) + DNN * (half + 1))
                nc.scalar.activation(yrow, bank[4][:, :], ACT.Copy).then_inc(yrow_ready, 1)

            with act.Fori(0, n) as r:
                with act.Fori(0, PAIRS) as i:
                    j = r * PAIRS + i
                    expert(j, 0)
                    expert(j, 1)
            keep_combT(n * (2 * PAIRS) + 1)
            for a in range(TT):
                act.wait_ge(comb_added, n * (4 * PAIRS) + (a + 2))
                squares(a).then_inc(sq_done, 1)

        @block.tensor
        def _(pe):
            mm = nc.tensor.matmul

            def turn(dst, src, rows=P):
                return nc.tensor.transpose(dst, src, ident[0:rows, 0:rows])

            pe.wait_ge(tables, 1)
            pe.wait_ge(prm_in, 16 * 4)
            turn(bank[0][:, 0:17], prm_rows, 17).then_inc(prmT_done, 1)
            for a in range(TT):
                pe.wait_ge(h_ready, a + 1)
                for k in range(KT):
                    c = T * (k % 2) + P * a
                    turn(bank[4 + k // 2][:, c:c + P], hmix[:, a, P * k:P * (k + 1)]).then_inc(hT_done, 1)

            def project(g, k):
                s = 4 * g + k // 2
                if k % 2 == 0:
                    pe.wait_ge(w_in_in[s], 16)
                base = D * (k % 2)
                b0 = 4 if g == 1 else 0
                last = None
                for m in range(8):
                    is_v = (g == 1 and m < 4) or (g == 2 and m >= 4)
                    if is_v:
                        continue
                    b, c = b0 + m // 2, T * (m % 2)
                    last = mm(bank[b][:, c:c + T], gu_ring[:, s, base + P * m:base + P * (m + 1)], hT[:, k, :],
                              start=(k == 0 and m % 2 == 0), stop=(k == KT - 1), skip_group_check=True)
                if g:
                    v0 = 0 if g == 1 else 512
                    for a in range(TT):
                        b = b0 + (0 if g == 1 else 2) + a
                        last = mm(bank[b][:, :], hT[:, k, P * a:P * (a + 1)],
                                  gu_ring[:, s, base + v0:base + v0 + 512], start=(k == 0), stop=(k == KT - 1))
                if k % 2:
                    last.then_inc(w_in_used, 1)

            pe.wait_ge(hT_ready_a, 1)
            pe.wait_ge(hT_ready_v, 1)
            pe.wait_ge(prm_ready, 1)
            for k in range(KT):
                project(0, k)
            for k in range(KT):
                project(1, k)

            def score(g):
                if g == 0:
                    pe.wait_ge(proj_ready_v, 2)
                    pe.wait_ge(proj_ready_a, 2)
                elif g == NH:
                    pe.wait_ge(proj_ready_v, 3)
                if g >= 1:
                    pe.wait_ge(scores_read, g)
                h = g % NH
                maps = 2 if g < NH else 1
                rows = HD // maps
                for m in range(maps):
                    r0 = HD * (h % 2) + rows * m
                    tq, tk = (h // 2, 4 + h // 2) if g < NH else (8 + h // 2, 12 + h // 2)
                    q, k = qkT[r0:r0 + rows, tq, :], qkT[r0:r0 + rows, tk, :]
                    mm(bank[4 + m][:, 0:T], q[:, P:T], k, start=True, stop=True)
                    last = mm(bank[4 + m][:, T:T + P], q[:, 0:P], k[:, 0:P], start=True, stop=True)
                last.then_inc(scores_done, 1)

            def turn_probs(g):
                pe.wait_ge(probs_ready, g + 1)
                if g >= 1:
                    pe.wait_ge(probsT_ready, g)
                for b in range(3):
                    last = turn(bank[6][:, P * b:P * (b + 1)], probs[g % 2][:, P * b:P * (b + 1)])
                last.then_inc(probsT_done, 1)

            def pv(g):
                pe.wait_ge(probsT_ready, g + 1)
                if g >= 1:
                    pe.wait_ge(pv_read, g)
                turned = sum(at <= g + 1 for at in TURN_AT)
                if turned:
                    pe.wait_ge(mixT_ready, turned)
                pt = probsT
                v = vS[:, :, HD * g:HD * (g + 1)]
                mm(bank[7][:, 0:HD], pt[:, T:T + P], v[:, 0, :], start=True, stop=True)
                mm(bank[7][:, HD:P], pt[:, 0:P], v[:, 0, :], start=True, stop=False)
                mm(bank[7][:, HD:P], pt[:, P:T], v[:, 1, :], start=False, stop=True).then_inc(pv_done, 1)

            def turn_mix(kt, g):
                if kt < NH // 2:
                    pe.wait_ge(mix_ready, kt + 1)
                pe.wait_ge(pv_read, g - 1)
                if kt >= 1:
                    pe.wait_ge(mixT_ready, kt)
                for a in range(TT):
                    last = turn(bank[7][:, P + P * a:2 * P + P * a], hmix[:, a, P * kt:P * (kt + 1)])
                last.then_inc(mixT_done, 1)

            def out_project(kt):
                pe.wait_ge(mixT_ready, kt + 1)
                if kt == 0:
                    pe.wait_ge(proj_ready_v, 3)
                    pe.wait_ge(proj_ready_a, 3)
                if kt % 2 == 0:
                    pe.wait_ge(w_out_in[kt // 2], 16)
                for a in range(TT):
                    for c in range(2):
                        w0 = D * (kt % 2) + 512 * c
                        last = mm(bank[2 * a + c][:, :], mixT[:, kt, P * a:P * (a + 1)],
                                  dn_ring[:, kt // 2, w0:w0 + 512], start=(kt == 0), stop=(kt == KT - 1))
                    if kt == KT - 1:
                        last.then_inc(x1_done, 1)
                if kt < KT - 1:
                    last.then_inc(oproj_done, 1)

            score(0)
            for g in range(2 * NH):
                if g >= 1:
                    turn_probs(g - 1)
                if g + 1 < 2 * NH:
                    score(g + 1)
                for k in GROUP_C_AT.get(g, ()):
                    project(2, k)
                if g in OUT_AT:
                    out_project(OUT_AT[g])
                if g in TURN_AT:
                    turn_mix(TURN_AT[g], g)
                if g >= 1:
                    pv(g - 1)
            turn_probs(2 * NH - 1)
            pv(2 * NH - 1)
            out_project(6)
            turn_mix(NH - 1, 2 * NH + 1)
            out_project(7)

            for a in range(TT):
                pe.wait_ge(x1_ready, a + 1)
                for k in range(KT):
                    c = T * (k % 2) + P * a
                    turn(bank[4 + k // 2][:, c:c + P], xres[:, a, P * k:P * (k + 1)]).then_inc(h2T_done, 1)
            pe.wait_ge(rw_in, 16)
            for k in range(KT):
                if k % 2 == 0:
                    pe.wait_ge((h2T_ready_v, h2T_ready_a)[k // 2 % 2], k // 4 + 1)
                c = NE * (k // 2)
                last = mm(bank[0][c:c + NE, 0:T], rw[:, k, :], h2T[:, k, :], start=(k % 2 == 0), stop=(k % 2 == 1),
                          skip_group_check=True)
            last.then_inc(logitsT_done, 1)
            pe.wait_ge(logitsT_ready, 1)
            for a in range(TT):
                last = turn(bank[1][:, P * a:P * (a + 1)], logitsT[:, P * a:P * (a + 1)])
            last.then_inc(logits_done, 1)
            pe.wait_ge(tri_made, 1)
            pe.wait_ge(chosen_ready, 1)
            mm(bank[2][:, 0:NE], tri, chosen[:, 0, :], start=True, stop=True)
            mm(bank[2][:, NE:2 * NE], ones, chosen[:, 0, :], start=True, stop=False)
            mm(bank[2][:, NE:2 * NE], tri, chosen[:, 1, :], start=False, stop=True)
            mm(bank[3][:, 0:NE], ones, chosen[:, 0, :], start=True, stop=False)
            mm(bank[3][:, 0:NE], ones, chosen[:, 1, :], start=False, stop=True).then_inc(pos_done, 1)

            def gather(v):
                pe.wait_ge(sel_ready, v)
                pe.wait_ge(h2_ready, TT)
                for k in range(KT):
                    b, c = 5 + k // 4, P * (k % 4)
                    for a in range(TT):
                        last = mm(bank[b][:, c:c + P], hmix[:, a, P * k:P * (k + 1)],
                                  sel[:, a, :, :].rearrange("p e n -> p (e n)"), start=(a == 0), stop=(a == TT - 1))
                last.then_inc(gather_done, 1)

            def turn_sel(v):
                pe.wait_ge(selg_ready, v)
                for a in range(TT):
                    last = turn(bank[7][:, P * a:P * (a + 1)], selg[:, a, :, :].rearrange("p e n -> p (e n)"))
                last.then_inc(selT_done, 1)

            def combine(a, b, v):
                pe.wait_ge(comb_added, v)
                for c in range(2):
                    rows = slice(CAP * c, CAP * (c + 1))
                    last = mm(bank[b + c][:, :], combT[rows, P * a:P * (a + 1)], yrow[rows, :], start=True, stop=True)
                last.then_inc(comb_done, 1)

            def add_bias(b, c, col):
                mm(bank[b][CAP * c:CAP * (c + 1), :], bias_sel[0:3 * NE, :], bias3[0:3 * NE, col:col + 512],
                   start=True, stop=False, skip_group_check=True)

            def gate_up(j, half):
                for k in range(KT):
                    s = 8 * half + k
                    pe.wait_ge(gu_in[s], j * 16 + 16)
                    for b in range(2):
                        for c in range(2):
                            w0 = FF * b + 512 * c
                            last = mm(bank[2 + b][CAP * c:CAP * (c + 1), :], xg[:, k, CAP * half:CAP * (half + 1)],
                                      gu_ring[:, s, w0:w0 + 512], start=False, stop=(k == KT - 1),
                                      skip_group_check=True)
                    last.then_inc(gu_used, 1)

            def down(j, half):
                for k in range(KT):
                    q = k // 2
                    if k % 2 == 0:
                        pe.wait_ge(dn_in[q], j * 32 + 16 * (half + 1))
                    a0 = P * (k % 4) + CAP * (k // 4)
                    for c in range(2):
                        w0 = D * (k % 2) + 512 * c
                        last = mm(bank[4][CAP * c:CAP * (c + 1), :], actT[:, a0:a0 + CAP], dn_ring[:, q, w0:w0 + 512],
                                  start=False, stop=(k == KT - 1), skip_group_check=True)
                    if k % 2:
                        last.then_inc(dn_used, 1)

            def expert(j, half):
                def nth(m, c):
                    return j * (2 * m) + (m * half + c)

                turn_sel(nth(1, 1))
                if half == 0:
                    pe.wait_ge(xg_ready, j + 1)
                pe.wait_ge(bias_sel_ready, nth(1, 1))
                for b in range(2):
                    for c in range(2):
                        add_bias(2 + b, c, FF * b + 512 * c)
                gate_up(j, half)
                pe.wait_ge(yrow_ready, nth(1, 1))
                for c in range(2):
                    add_bias(4, c, 2 * FF + 512 * c)
                pe.wait_ge(combT_ready, nth(1, 1))
                combine(0, 0, nth(2, 1))
                if half == 0:
                    combine(1, 5, nth(2, 1))
                else:
                    gather(j + 2)
                    combine(1, 0, nth(2, 2))
                pe.wait_ge(act_ready, nth(1, 1))
                for c in range(4):
                    last = turn(bank[7][:, P * c:P * (c + 1)], act_t[:, P * c:P * (c + 1)])
                last.then_inc(actT_done, 1)
                pe.wait_ge(actT_ready, nth(1, 1))
                down(j, half)

            gather(1)
            pe.wait_ge(rounds_ready, 1)
            n = pe.value_load(rounds[0:1, 0:1], min_val=1, max_val=ROUNDS)
            with pe.Fori(0, n) as r:
                with pe.Fori(0, PAIRS) as i:
                    j = r * PAIRS + i
                    expert(j, 0)
                    expert(j, 1)
            turn_sel(n * (2 * PAIRS) + 1)
            pe.wait_ge(yrow_ready, n * (2 * PAIRS) + 1)
            pe.wait_ge(combT_ready, n * (2 * PAIRS) + 1)
            combine(0, 0, n * (4 * PAIRS) + 1)
            combine(1, 5, n * (4 * PAIRS) + 1)

        @block.vector
        def _(dve):
            V = nc.vector
            count = [0]

            def link(ins):
                count[0] += 1
                ins.then_inc(dve_step, 1)
                dve.wait_ge(dve_step, count[0])

            dve.wait_ge(tables, 6)
            V.memset(st[:, 62:63], -0.5).then_inc(consts, 1)
            link(V.tensor_scalar(mod_int, dist_int, 3, None, ALU.bitwise_and))
            link(V.tensor_scalar(dist_dil, mod_int, 0.0, None, ALU.is_equal))
            link(V.scalar_tensor_tensor(out=mult, in0=dist_diff, scalar=128.0, in1=dist_dil, op0=ALU.is_le, op1=ALU.add))
            link(V.tensor_scalar(mod_int, dist_int, 15, None, ALU.bitwise_and))
            link(V.tensor_scalar(dist_dil, mod_int, 0.0, None, ALU.is_equal))
            link(V.tensor_tensor(mult, mult, dist_dil, ALU.add))
            link(V.scalar_tensor_tensor(out=mult, in0=dist_diff, scalar=0.0, in1=mult, op0=ALU.is_ge, op1=ALU.mult))
            link(V.tensor_scalar(dist_dil, mult, 0.0, FAR, ALU.is_equal, ALU.mult))
            link(V.tensor_tensor(dist_dil, dist_dil, dist_diff, ALU.max))

            def mean_square(rs_count, sums, value):
                dve.wait_ge(sums, value)
                V.tensor_scalar(st[:, 0:2], st[:, 0:2], 1.0 / D, EPS, ALU.mult, ALU.add).then_inc(ms_ready, 1)
                dve.wait_ge(rs_ready, rs_count)

            dve.wait_ge(x_in, 16 * TT)
            mean_square(1, sq_done, 1)
            for a in range(TT):
                V.tensor_scalar(hmix[:, a, :], xres[:, a, :], st[:, 2 + a:3 + a], None, ALU.mult).then_inc(h_ready, 1)

            dve.wait_ge(prmT_done, 1)
            link(V.tensor_copy(prm[:, :], bank[0][:, 0:17]))
            V.tensor_scalar(prm[:, 16:17], prm[:, 16:17], 1.0 - LAM_INIT, None, ALU.mult).then_inc(prm_ready, 1)
            dve.wait_ge(prm_ready, 1)
            dve.wait_ge(hT_done, 2 * KT)
            for k in (0, 1, 4, 5):
                last = V.tensor_scalar(hT[:, k, :], bank[4 + k // 2][:, T * (k % 2):T * (k % 2 + 1)], prm[:, k:k + 1],
                                       None, ALU.mult)
            last.then_inc(hT_ready_v, 1)
            dve.wait_ge(w_in_used, 4)
            for b in range(2):
                last = V.tensor_copy(qkT[:, 4 + 2 * b:6 + 2 * b, :].rearrange("p m t -> p (m t)"), bank[2 + b][:, :])
            last.then_inc(proj_ready_v, 1)
            dve.wait_ge(small_in, 16 * 5)
            for i in range(2):
                ins = V.tensor_tensor_reduce(out=lam_rows[:, 2 * i, :], in0=lam_rows[:, 2 * i, :],
                                             in1=lam_rows[:, 2 * i + 1, :], scale=1.0, scalar=0.0,
                                             op0=ALU.mult, op1=ALU.add, accum_out=st[:, 4 + i:5 + i])
                if i == 0:
                    link(ins)
            ins.then_inc(lam_sum, 1)
            dve.wait_ge(bias_in, 16 * 6)
            link(V.tensor_copy(bias3[0:3 * NE, :], bias_rows[0:3 * NE, :]))
            for q in (1, 2):
                rows = slice(NE * q, NE * (q + 1))
                src = bias_rows
                for step in range(q):
                    link(V.tensor_tensor(bias_rest[rows, :], src[rows, :], bias3[rows, :], ALU.subtract))
                    ins = V.tensor_copy(bias3[rows, :], bias_rest[rows, :])
                    src = bias_rest
                    if (q, step) != (2, 1):
                        link(ins)
            ins.then_inc(bias_split, 1)
            dve.wait_ge(lam_exp, 1)
            link(V.tensor_tensor(st[:, 8:9], st[:, 6:7], st[:, 7:8], ALU.subtract))
            link(V.tensor_scalar(st[:, 8:9], st[:, 8:9], LAM_INIT, None, ALU.add))
            dve.wait_ge(w_in_used, 8)
            for a in range(TT):
                last = V.tensor_copy(vS[:, a, 0:512], bank[4 + a][:, :])
            last.then_inc(proj_ready_v, 1)

            def negated_scores(g):
                dve.wait_ge(scores_done, g + 1)
                slope = SLOPES[2 * (g % NH) + (g >= NH)]
                dist = dist_diff if g < NH else dist_dil
                maps = 2 if g < NH else 1
                s = scores[g % 2]
                V.scalar_tensor_tensor(out=s[:, 0:maps, :], in0=dist.unsqueeze(1).broadcast_to([P, maps, T + P]),
                                       scalar=slope, in1=psum[:, 4:4 + maps, 0:T + P], op0=ALU.mult,
                                       op1=ALU.subtract).then_inc(scores_read, 1)
                dve.wait_ge(scores_read, g + 1)
                for c, w, i in ((0, T, 2), (T, P, 0)):
                    lo = 24 + 4 * (g % 2) + i
                    ins = V.tensor_reduce(st[:, lo:lo + maps], s[:, 0:maps, c:c + w], AX.X, ALU.min)
                ins.then_inc(max_ready, 1)

            def diff_probs(g):
                dve.wait_ge(exp_done, g + 1)
                s, pr = scores[g % 2], probs[g % 2]
                link(V.reciprocal(st[:, 56:60], st[:, 32 + 4 * (g % 2):36 + 4 * (g % 2)]))
                link(V.tensor_scalar(st[:, 57:60:2], st[:, 57:60:2], st[:, 8:9], None, ALU.mult))
                for c, w, z in ((0, T, 58), (T, P, 56)):
                    p1, p2 = s[:, 0, c:c + w], s[:, 1, c:c + w]
                    link(V.tensor_scalar(p2, p2, st[:, z + 1:z + 2], None, ALU.mult))
                    ins = V.scalar_tensor_tensor(out=pr[:, c:c + w], in0=p1, scalar=st[:, z:z + 1], in1=p2,
                                                 op0=ALU.mult, op1=ALU.subtract)
                ins.then_inc(probs_ready, 1)

            def dil_probs(g):
                dve.wait_ge(exp_done, g + 1)
                dve.wait_ge(probs_ready, g)
                s, pr = scores[g % 2], probs[g % 2]
                if g >= NH + 2:
                    dve.wait_ge(pv_read, g - 1)
                z = 40 + 2 * (g % 2)
                for c, w, a in ((0, T, 1), (T, P, 0)):
                    link(V.scalar_tensor_tensor(out=pr[:, c:c + w], in0=s[:, 0, c:c + w], scalar=1.0,
                                                in1=mult[:, c:c + w], op0=ALU.mult, op1=ALU.mult,
                                                accum_out=st[:, 50 + a:51 + a]))
                V.reciprocal(st[:, z:z + 2], st[:, 50:52]).then_inc(probs_ready, 1)

            def norm_pair(kt):
                dve.wait_ge(pv_read, 2 * kt + 2)
                hv = hmix[:, :, P * kt:P * (kt + 1)]
                sq = posm[:, :, 0:P]
                link(V.tensor_tensor(sq, hv, hv, ALU.mult))
                link(V.tensor_reduce(st[:, 12:16].rearrange("p (a h) -> p a h", a=TT),
                                     sq.rearrange("p a (h d) -> p a h d", d=HD), AX.X, ALU.add))
                V.tensor_scalar(st[:, 16:20], st[:, 12:16], 1.0 / HD, EPS, ALU.mult, ALU.add).then_inc(ms_ready, 1)
                dve.wait_ge(rs_ready, 2 + kt)
                hv4 = hv.rearrange("p a (h d) -> p a h d", d=HD)
                rs = st[:, 20:24].rearrange("p (a h) -> p a h", a=TT).unsqueeze(3).broadcast_to([P, TT, 2, HD])
                V.tensor_tensor(hv4, hv4, rs, ALU.mult).then_inc(mix_ready, 1)

            link(V.tensor_scalar(scores[0][:, 0, :], dist_diff, 0.0, FAR, ALU.is_lt, ALU.mult))
            link(V.tensor_tensor(dist_diff, dist_diff, scores[0][:, 0, :], ALU.max))
            negated_scores(0)
            for g in range(2 * NH):
                if g + 1 < 2 * NH:
                    negated_scores(g + 1)
                if g < NH:
                    diff_probs(g)
                else:
                    dil_probs(g)
                if g >= 3 and g % 2 == 1 and g <= NH + 1:
                    norm_pair((g - 3) // 2)
                if g == NH - 2:
                    dve.wait_ge(w_in_used, 12)
                    for b in range(2):
                        last = V.tensor_copy(qkT[:, 12 + 2 * b:14 + 2 * b, :].rearrange("p m t -> p (m t)"), bank[b][:, :])
                    last.then_inc(proj_ready_v, 1)

            for a in range(TT):
                dve.wait_ge(x1_done, a + 1)
                xs = xres[:, a, :].rearrange("p (c n) -> p c n", c=2)
                V.tensor_tensor(xs, xs, psum[:, 2 * a:2 * a + 2, :], ALU.add).then_inc(x1_ready, 1)
            ffn_w = prm[:, 8:16]
            link(V.tensor_copy(iota_e, iota[:, 0:NE]))
            link(V.memset(posm[:, :, :], -1.0))
            dve.wait_ge(h2T_done, 2 * KT)
            for b in (0, 2):
                V.tensor_tensor(h2T[:, 2 * b:2 * b + 2, :], bank[4 + b][:, :].rearrange("p (k t) -> p k t", k=2),
                                ffn_w[:, 2 * b:2 * b + 2].unsqueeze(2).broadcast_to([P, 2, T]), ALU.mult)\
                    .then_inc(h2T_ready_v, 1)
            mean_square(2 + NH // 2, sq_done, 2)
            dve.wait_ge(logitsT_done, 1)
            V.tensor_copy(logitsT, bank[0][:, 0:T]).then_inc(logitsT_ready, 1)
            for a in range(TT):
                V.tensor_scalar(hmix[:, a, :], xres[:, a, :], st[:, 2 + a:3 + a], None, ALU.mult).then_inc(h2_ready, 1)
            dve.wait_ge(logits_done, 1)
            link(V.tensor_reduce(logits, bank[1][:, 0:T].rearrange("p (a s e) -> p a e s", a=TT, s=4), AX.X, ALU.add))
            for a in range(TT):
                link(V.scalar_tensor_tensor(out=logits[:, a, :], in0=logits[:, a, :], scalar=st[:, 2 + a:3 + a],
                                            in1=rb[:, :], op0=ALU.mult, op1=ALU.add))
            for a in range(TT):
                link(V.max(top_v[:, a, :], logits[:, a, :]))
            V.tensor_scalar(st[:, 46:48], top_v[:, :, 0], -1.0, None, ALU.mult).then_inc(top_ready, 1)
            for a in range(TT):
                link(V.max_index(top_i[:, a, :], top_v[:, a, :], logits[:, a, :]))
            link(V.tensor_copy(top_f, top_i))
            wide = [P, TT, TOPK, NE]
            link(V.tensor_tensor(sel_k, iota_e.unsqueeze(1).unsqueeze(1).broadcast_to(wide),
                                 top_f[:, :, 0:TOPK].unsqueeze(3).broadcast_to(wide), ALU.is_equal))
            V.tensor_reduce(chosen, sel_k.rearrange("p a k e -> p a e k"), AX.X, ALU.add).then_inc(chosen_ready, 1)
            dve.wait_ge(top_exp, 1)
            link(V.reciprocal(st[:, 52:54], st[:, 48:50]))
            link(V.tensor_tensor(top_e[:, :, 0:TOPK], top_e[:, :, 0:TOPK],
                                 st[:, 52:54].unsqueeze(2).broadcast_to([P, TT, TOPK]), ALU.mult))
            link(V.tensor_tensor(selg_k, sel_k, top_e[:, :, 0:TOPK].unsqueeze(3).broadcast_to(wide), ALU.mult))
            link(V.tensor_reduce(gates[:, :, 2:2 + NE], selg_k.rearrange("p a k e -> p a e k"), AX.X, ALU.add))
            link(V.tensor_copy(gates[:, :, 0:2], gates[:, :, NE:NE + 2]))
            dve.wait_ge(pos_done, 1)
            link(V.scalar_tensor_tensor(out=slot0, in0=bank[2][:, 0:2 * NE].rearrange("p (a e) -> p a e", a=TT),
                                        scalar=1.0, in1=chosen, op0=ALU.add, op1=ALU.mult))
            link(V.tensor_scalar(posm[:, :, 2:2 + NE], slot0, 1.0, None, ALU.subtract))
            four = [P, TT, 2, CAP]

            def one_hot(dst, c, n):
                return V.tensor_tensor(dst, posm[:, :, bass.ds(c, n)].unsqueeze(3).broadcast_to(four),
                                       iota[:, :].unsqueeze(1).unsqueeze(1).broadcast_to(four), ALU.is_equal)

            def choose(pos_c, gate_c, e, chain):
                chain(one_hot(selg, pos_c, 1))
                V.tensor_tensor(selg, selg, gates[:, :, bass.ds(gate_c, 1)].unsqueeze(3).broadcast_to(four),
                                ALU.mult).then_inc(selg_ready, 1)
                V.tensor_copy(bias_sel[0:3 * NE, :], expert_of[0:3 * NE, bass.ds(e, 1)].broadcast_to([3 * NE, CAP]))\
                    .then_inc(bias_sel_ready, 1)

            def keep_xg(v):
                dve.wait_ge(gather_done, v)
                V.tensor_tensor(xg, psum[:, 5:7, :].rearrange("p b (k n) -> p (b k) n", k=4),
                                ffn_w.unsqueeze(2).broadcast_to([P, KT, P]), ALU.mult).then_inc(xg_ready, 1)

            one_hot(sel, 2, 2).then_inc(sel_ready, 1)
            for r in range(1, ROUNDS):
                link(V.tensor_scalar(posm[:, :, 2 + NE * r:2 + NE * (r + 1)], slot0, 1.0 + CAP * r, None, ALU.subtract))
            link(V.reduce_max(st[:, 54:55], bank[3][:, 0:NE], AX.X))
            link(V.tensor_scalar(st[:, 55:56], st[:, 54:55], float(CAP), 1.0, ALU.is_gt, ALU.add))
            for r in range(2, ROUNDS):
                link(V.scalar_tensor_tensor(out=st[:, 55:56], in0=st[:, 54:55], scalar=float(CAP * r), in1=st[:, 55:56],
                                            op0=ALU.is_gt, op1=ALU.add))
            V.tensor_copy(rounds[:, :], st[:, 55:56]).then_inc(rounds_ready, 1)
            V.tensor_scalar(more_rounds[:, :], st[:, 55:56], 1.0, None, ALU.subtract).then_inc(rounds_ready, 1)
            V.memset(yrow, 0.0).then_inc(yrow_ready, 1)
            V.memset(st[:, 60:61], 0.0).then_inc(comb_added, 1)
            link(V.tensor_reduce(expert_of[:, 0:NE], ident[:, 0:3 * NE].rearrange("p (q e) -> p e q", q=3), AX.X, ALU.add))
            link(V.tensor_copy(expert_of[:, NE:NE + 1], expert_of[:, 0:1]))
            choose(1, 1, 0, link)
            keep_xg(1)
            dve.wait_ge(rounds_ready, 1)
            n = dve.value_load(rounds[0:1, 0:1], min_val=1, max_val=ROUNDS)

            STEPS = 4

            def add_combined(a, b, v):
                dve.wait_ge(comb_done, v)
                xs = xres[:, a, :].rearrange("p (c n) -> p c n", c=2)
                V.tensor_tensor(xs, xs, psum[:, b:b + 2, :], ALU.add).then_inc(comb_added, 1)

            def expert(j, i, half, chain):
                def nth(m, c):
                    return j * (2 * m) + (m * half + c)

                if half == 0:
                    dve.wait_ge(gather_done, j + 1)
                    one_hot(sel, j * 2 + 4, 2).then_inc(sel_ready, 1)
                dve.wait_ge(gu_used, nth(KT, KT))
                V.tensor_scalar(gate_t, bank[2][:, :], LIMIT, None, ALU.min).then_inc(gate_ready, 1)
                chain(V.tensor_scalar(up_t, bank[3][:, :], -LIMIT, LIMIT, ALU.max, ALU.min))
                dve.wait_ge(gate_ready, nth(1, 1))
                V.scalar_tensor_tensor(out=up_t, in0=up_t, scalar=1.0, in1=gate_t, op0=ALU.add, op1=ALU.mult)\
                    .then_inc(lin_ready, 1)
                dve.wait_ge(lin_ready, nth(1, 1))
                dve.wait_ge(sig_ready, nth(1, 1))
                V.tensor_tensor(act_t, up_t, sig_t, ALU.mult).then_inc(act_ready, 1)
                add_combined(0, 0, nth(2, 1))
                choose(j * 2 + (half + 2), i * 2 + (half + 2), i * 2 + (half + 1), chain)
                if half == 0:
                    add_combined(1, 5, nth(2, 2))
                else:
                    keep_xg(j + 2)
                    add_combined(1, 0, nth(2, 2))

            with dve.Fori(0, n) as r:
                with dve.Fori(0, PAIRS) as i:
                    j = r * PAIRS + i
                    at = [0]

                    def chain(ins):
                        at[0] += 1
                        ins.then_inc(dve_loop, 1)
                        dve.wait_ge(dve_loop, j * STEPS + at[0])

                    expert(j, i, 0, chain)
                    expert(j, i, 1, chain)
                    assert at[0] == STEPS, at[0]
            last_x = n * (2 * PAIRS)
            add_combined(0, 0, last_x * 2 + 1)
            add_combined(1, 5, last_x * 2 + 2)
            dve.wait_ge(fw_in, 16)
            for a in range(TT):
                dve.wait_ge(sq_done, 3 + a)
                V.tensor_scalar(st[:, a:a + 1], st[:, a:a + 1], 1.0 / D, EPS, ALU.mult, ALU.add).then_inc(ms_ready, 1)
                dve.wait_ge(rs_ready, 3 + NH // 2 + a)
                V.scalar_tensor_tensor(out=hmix[:, a, :], in0=xres[:, a, :], scalar=st[:, 2 + a:3 + a],
                                       in1=gu_ring[:, 0, 0:D], op0=ALU.mult, op1=ALU.mult).then_inc(h_ready, 1)


_INS = ['x', 'attn_norm_w', 'w_in', 'diff_lambda_q1', 'diff_lambda_k1', 'diff_lambda_q2', 'diff_lambda_k2',
        'diff_subln_w', 'w_out', 'ffn_norm_w', 'router_w', 'router_b', 'w_gate_up', 'b_gate_up', 'w_down', 'b_down',
        'final_norm_w']


def kernel(**inputs):
    import concourse.bacc as _bacc
    from concourse.bass_utils import run_bass_kernel_spmd as _run

    nc = _bacc.Bacc("TRN2", target_bir_lowering=False, num_devices=1)
    arrays, args = {}, []
    for name in _INS:
        a = np.ascontiguousarray(inputs[name])
        arrays[f"in_{name}_dram"] = a
        args.append(nc.dram_tensor(f"in_{name}_dram", a.shape, mybir.dt.from_np(a.dtype), kind="ExternalInput").ap())
    out = nc.dram_tensor("out_0_dram", (1, T, D), F32, kind="ExternalOutput").ap()
    moe_block(nc, *args, out)
    r = _run(nc, [arrays], core_ids=[0])
    return r.results[0]["out_0_dram"]
```
